# Optimizing a Trainium2 kernel written in Bass

```python
import math
import jax, jax.numpy as jnp
from jax import lax
import numpy as np

D_MODEL = 1024
BATCH = 1
SEQ = 512
DEPTH = 1

GDN_HEADS = 8
GDN_HEAD_DIM = 128
GDN_WIDTH = GDN_HEADS * GDN_HEAD_DIM
GDN_CONV = 4
GDN_CHUNK = 64
SC_WIDTH = D_MODEL
SC_CONV = 3
N_EXPERTS = 32
TOP_K = 4
D_FF = D_MODEL
SWIGLU_LIMIT = 7.0
SWIGLU_ALPHA = 1.702
MOE_BLOCK = 128
NORM_EPS = 1e-6
IN_SPLITS = (3 * GDN_WIDTH, GDN_WIDTH, GDN_HEADS, GDN_HEADS, SC_WIDTH, SC_WIDTH, SC_WIDTH, D_MODEL, D_MODEL)
D_IN = 4 * GDN_WIDTH + 2 * GDN_HEADS + 3 * SC_WIDTH + 2 * D_MODEL

kernel_name = 'hybrid_gdn_shortconv_moe_block'

def rms_norm(x, g):
    xf = x.astype(jnp.float32)
    y = xf * lax.rsqrt(jnp.mean(xf * xf, axis=-1, keepdims=True) + NORM_EPS)
    return (y * g.astype(jnp.float32)).astype(x.dtype)

def l2_normalize(x):
    xf = x.astype(jnp.float32)
    return xf * lax.rsqrt(jnp.sum(xf * xf, axis=-1, keepdims=True) + NORM_EPS)

def causal_depthwise_conv(x, w):
    K = w.shape[0]
    S = x.shape[1]
    xp = jnp.pad(x, ((0, 0), (K - 1, 0), (0, 0)))
    y = w[0] * xp[:, 0:S]
    for j in range(1, K):
        y = y + w[j] * xp[:, j:j + S]
    return y

def gated_delta_rule_chunked(q, k, v, g, beta):
    Bn, S, H, Dk = q.shape
    Dv = v.shape[-1]
    C = GDN_CHUNK
    N = S // C

    def chunks(t):
        t = t.reshape((Bn, N, C, H) + t.shape[3:])
        return jnp.moveaxis(t, (1, 3), (0, 2))

    q = chunks(q) * (Dk ** -0.5)
    k = chunks(k)
    v = chunks(v)
    g = chunks(g)
    beta = chunks(beta)
    gcum = jnp.cumsum(g, axis=-1)
    idx = jnp.arange(C)
    causal = idx[:, None] >= idx[None, :]
    strict = idx[:, None] > idx[None, :]
    diff = gcum[..., :, None] - gcum[..., None, :]
    decay = jnp.where(causal, jnp.exp(jnp.where(causal, diff, 0.0)), 0.0)
    kb = k * beta[..., None]
    Lm = jnp.where(strict, jnp.einsum('nbhid,nbhjd->nbhij', kb, k) * decay, 0.0)
    eye = jnp.eye(C, dtype=Lm.dtype)
    T = lax.linalg.triangular_solve(Lm + eye, jnp.broadcast_to(eye, Lm.shape),
                                    left_side=True, lower=True, unit_diagonal=True)
    u = T @ (v * beta[..., None])
    w = T @ (kb * jnp.exp(gcum)[..., None])
    aqk = jnp.einsum('nbhid,nbhjd->nbhij', q, k) * decay
    qg = q * jnp.exp(gcum)[..., None]
    g_last = gcum[..., -1]
    kd = k * jnp.exp(g_last[..., None] - gcum)[..., None]

    def step(state, inp):
        w_n, u_n, qg_n, aqk_n, kd_n, gl_n = inp
        v_new = u_n - w_n @ state
        o_n = qg_n @ state + aqk_n @ v_new
        state = state * jnp.exp(gl_n)[..., None, None] + jnp.einsum('bhck,bhcv->bhkv', kd_n, v_new)
        return state, o_n

    state0 = jnp.zeros((Bn, H, Dk, Dv), jnp.float32)
    _, o = lax.scan(step, state0, (w, u, qg, aqk, kd, g_last))
    return jnp.moveaxis(o, (0, 2), (1, 3)).reshape(Bn, S, H, Dv)

def hybrid_mixer(xn, w_in, gdn_conv_w, gdn_A_log, gdn_dt_bias, gdn_norm_g, w_o_gdn,
                 sconv_w, w_o_sconv, w_mix_out):
    Bn, S, _ = xn.shape
    proj = xn @ w_in
    offsets = np.cumsum(IN_SPLITS)[:-1].tolist()
    qkv, z, a, b, xs, gate_b, gate_c, gate_A, gate_B = jnp.split(proj, offsets, axis=-1)

    qkv = jax.nn.silu(causal_depthwise_conv(qkv, gdn_conv_w))
    q, k, v = jnp.split(qkv, 3, axis=-1)
    q = l2_normalize(q.reshape(Bn, S, GDN_HEADS, GDN_HEAD_DIM))
    k = l2_normalize(k.reshape(Bn, S, GDN_HEADS, GDN_HEAD_DIM))
    v = v.reshape(Bn, S, GDN_HEADS, GDN_HEAD_DIM).astype(jnp.float32)
    beta = jax.nn.sigmoid(b.astype(jnp.float32))
    g = -jnp.exp(gdn_A_log.astype(jnp.float32)) * jax.nn.softplus(
        a.astype(jnp.float32) + gdn_dt_bias.astype(jnp.float32))
    o = gated_delta_rule_chunked(q, k, v, g, beta).astype(xn.dtype)
    o = rms_norm(o, gdn_norm_g) * jax.nn.silu(z.reshape(Bn, S, GDN_HEADS, GDN_HEAD_DIM))
    y_a = o.reshape(Bn, S, GDN_WIDTH) @ w_o_gdn

    y_b = (gate_b * causal_depthwise_conv(gate_c * xs, sconv_w)) @ w_o_sconv

    merged = jax.nn.sigmoid(gate_A) * y_a + jax.nn.sigmoid(gate_B) * y_b
    return merged @ w_mix_out

def moe_ffn(xn, w_router, b_router, w_gate_up, b_gate_up, w_down, b_down):
    Bn, S, D = xn.shape
    Tn = Bn * S
    TK = Tn * TOP_K
    xf = xn.reshape(Tn, D)
    logits = xf.astype(jnp.float32) @ w_router.astype(jnp.float32) + b_router.astype(jnp.float32)
    top_vals, top_idx = lax.top_k(logits, TOP_K)
    top_w = jax.nn.softmax(top_vals, axis=-1).astype(xn.dtype)

    e_flat = top_idx.reshape(-1)
    tok_flat = jnp.arange(TK, dtype=jnp.int32) // TOP_K
    order = jnp.argsort(e_flat)
    e_sorted = e_flat[order]
    tok_sorted = tok_flat[order]
    w_sorted = top_w.reshape(-1)[order]
    counts = jnp.bincount(e_flat, length=N_EXPERTS)
    start = jnp.cumsum(counts) - counts
    pcounts = ((counts + MOE_BLOCK - 1) // MOE_BLOCK) * MOE_BLOCK
    pend = jnp.cumsum(pcounts)
    pstart = pend - pcounts
    dest = pstart[e_sorted] + (jnp.arange(TK, dtype=jnp.int32) - start[e_sorted])
    n_blocks = (TK + N_EXPERTS * (MOE_BLOCK - 1) + MOE_BLOCK - 1) // MOE_BLOCK
    x_pad = jnp.zeros((n_blocks * MOE_BLOCK, D), xn.dtype).at[dest].set(xf[tok_sorted])
    block_e = jnp.minimum(jnp.searchsorted(pend, jnp.arange(n_blocks) * MOE_BLOCK, side='right'),
                          N_EXPERTS - 1)

    def expert_block(args):
        xb, e = args
        gu = xb @ w_gate_up[e] + b_gate_up[e]
        gate = jnp.minimum(gu[:, :D_FF], SWIGLU_LIMIT)
        up = jnp.clip(gu[:, D_FF:], -SWIGLU_LIMIT, SWIGLU_LIMIT)
        hid = (up + 1.0) * gate * jax.nn.sigmoid(SWIGLU_ALPHA * gate)
        return hid @ w_down[e] + b_down[e]

    y_blocks = lax.map(expert_block, (x_pad.reshape(n_blocks, MOE_BLOCK, D), block_e))
    y_sorted = y_blocks.reshape(n_blocks * MOE_BLOCK, D)[dest]
    out = jnp.zeros((Tn, D), xn.dtype).at[tok_sorted].add(y_sorted * w_sorted[:, None])
    return out.reshape(Bn, S, D)

def setup_inputs(seed: int = 0) -> dict:
    key = jax.random.key(seed)
    ks = jax.random.split(key, 20)
    f32 = jnp.float32
    L = DEPTH

    def nrm(k, shape, fan_in):
        return jax.random.normal(k, shape, f32) * (fan_in ** -0.5)

    def gain(k, shape):
        return 1.0 + 0.02 * jax.random.normal(k, shape, f32)

    def small(k, shape):
        return 0.01 * jax.random.normal(k, shape, f32)

    dt = jnp.exp(jax.random.uniform(ks[6], (L, GDN_HEADS), f32, math.log(1e-3), math.log(1e-1)))
    return {
        'x': jax.random.normal(ks[0], (BATCH, SEQ, D_MODEL), f32),
        'norm_mix_g': gain(ks[1], (L, D_MODEL)),
        'w_in': nrm(ks[2], (L, D_MODEL, D_IN), D_MODEL),
        'gdn_conv_w': nrm(ks[3], (L, GDN_CONV, 3 * GDN_WIDTH), GDN_CONV),
        'gdn_A_log': jnp.log(jax.random.uniform(ks[4], (L, GDN_HEADS), f32, 1.0, 16.0)),
        'gdn_dt_bias': dt + jnp.log(-jnp.expm1(-dt)),
        'gdn_norm_g': gain(ks[5], (L, GDN_HEAD_DIM)),
        'w_o_gdn': nrm(ks[7], (L, GDN_WIDTH, D_MODEL), GDN_WIDTH),
        'sconv_w': nrm(ks[8], (L, SC_CONV, SC_WIDTH), SC_CONV),
        'w_o_sconv': nrm(ks[9], (L, SC_WIDTH, D_MODEL), SC_WIDTH),
        'w_mix_out': nrm(ks[10], (L, D_MODEL, D_MODEL), D_MODEL),
        'norm_ffn_g': gain(ks[11], (L, D_MODEL)),
        'w_router': nrm(ks[12], (L, D_MODEL, N_EXPERTS), D_MODEL),
        'b_router': small(ks[13], (L, N_EXPERTS)),
        'w_gate_up': nrm(ks[14], (L, N_EXPERTS, D_MODEL, 2 * D_FF), D_MODEL),
        'b_gate_up': small(ks[15], (L, N_EXPERTS, 2 * D_FF)),
        'w_down': nrm(ks[16], (L, N_EXPERTS, D_FF, D_MODEL), D_FF),
        'b_down': small(ks[17], (L, N_EXPERTS, D_MODEL)),
        'norm_final_g': gain(ks[18], (D_MODEL,)),
    }

def reference(x, norm_mix_g, w_in, gdn_conv_w, gdn_A_log, gdn_dt_bias, gdn_norm_g, w_o_gdn,
              sconv_w, w_o_sconv, w_mix_out, norm_ffn_g, w_router, b_router, w_gate_up,
              b_gate_up, w_down, b_down, norm_final_g):
    h = x
    for l in range(DEPTH):
        h = h + hybrid_mixer(rms_norm(h, norm_mix_g[l]), w_in[l], gdn_conv_w[l], gdn_A_log[l],
                             gdn_dt_bias[l], gdn_norm_g[l], w_o_gdn[l], sconv_w[l], w_o_sconv[l],
                             w_mix_out[l])
        h = h + moe_ffn(rms_norm(h, norm_ffn_g[l]), w_router[l], b_router[l], w_gate_up[l],
                        b_gate_up[l], w_down[l], b_down[l])
    return rms_norm(h, norm_final_g)


_drawn_inputs = setup_inputs


def setup_inputs(seed=0):
    import zlib

    import numpy as np

    out = dict(_drawn_inputs(seed))
    spreads = {}
    factors = {'b_gate_up': 8.0, 'b_down': 8.0, 'norm_final_g': 2.911}
    for name, (base, spread) in spreads.items():
        noise = np.random.default_rng([zlib.crc32(name.encode()), seed]).standard_normal(out[name].shape)
        drawn = base * np.exp(spread * noise) if base else spread * noise
        out[name] = __import__('jax').numpy.asarray(drawn.astype(out[name].dtype))
    for name, factor in factors.items():
        out[name] = (out[name] * factor).astype(out[name].dtype)
    return out
```

```python
from contextlib import ExitStack

import concourse.bass as bass
from concourse import mybir

ALU = mybir.AluOpType
ACT = mybir.ActivationFunctionType
AX = mybir.AxisListType.X
F32 = mybir.dt.float32
F32R = mybir.dt.float32r
I32 = mybir.dt.int32
U32 = mybir.dt.uint32

P = 128
SPLIT_PASSES = 3


def wait(eng, sem, value):
    if not isinstance(value, int) or value > 0:
        eng.wait_ge(sem, value)


def col(ap):
    return ap.rearrange("(n a) -> n a", a=1)


def hybrid_block(nc, x, norm_mix_g, w_in, gdn_conv_w, gdn_A_log, gdn_dt_bias, gdn_norm_g, w_o_gdn,
                 sconv_w, w_o_sconv, w_mix_out, norm_ffn_g, w_router, b_router, w_gate_up,
                 b_gate_up, w_down, b_down, norm_final_g, out):
    _, SEQ, D = x.shape
    TT = SEQ // P
    KD = D // P
    HEADS = gdn_A_log.shape[1]
    QKV = gdn_conv_w.shape[2] // P
    CONV = gdn_conv_w.shape[1]
    SCONV = sconv_w.shape[1]
    E = w_router.shape[2]
    TOPK = 4
    EPS = 1e-6
    GW = 512
    GT = GW // P
    assert QKV == 3 * HEADS and D == 2 * GW and KD == 8

    x_d = x[0].rearrange("(t p) d -> p t d", p=P)
    out_d = out[0].rearrange("(t p) d -> p t d", p=P)
    w_in_d = w_in[0]
    Z0 = QKV * P
    A0 = Z0 + D
    B0 = A0 + HEADS
    XS0 = B0 + HEADS
    GB0, GC0, GA0, GBB0 = XS0 + D, XS0 + 2 * D, XS0 + 3 * D, XS0 + 4 * D

    xn2_d = nc.dram_tensor("xn2_scratch", (SEQ, D), F32, kind="Internal").ap()

    with ExitStack() as ctx:
        def sem(name):
            return ctx.enter_context(nc.semaphore(name))

        mixer_sems = []

        def mixer_sem(name):
            mixer_sems.append(nc.alloc_semaphore(name=name))
            return mixer_sems[-1]

        def keep(name, shape, dt=F32):
            return ctx.enter_context(nc.sbuf_tensor(name, shape, dt))

        ident = keep("ident", [P, P])
        tri = keep("tri", [P, P])
        strict = keep("strict", [P, P])
        LEVELS = 7
        pair_mask = keep("pair_mask", [P, LEVELS, P])
        cols = keep("cols", [P, P])
        gdn_gain = keep("gdn_gain", [P, 1])
        ab = keep("ab", [P, SEQ])
        decay_rate = keep("decay_rate", [P, 1])
        dt_bias = keep("dt_bias", [P, 1])
        zT = keep("zT", [P, HEADS, SEQ])
        logits = keep("logits", [P, TT, E])

        def conv_tap(j, c):
            return cols[:, j * QKV + c:j * QKV + c + 1]

        def sconv_tap(j, c):
            n = CONV * QKV + j * KD + c
            return cols[:, n:n + 1]

        def mix_gain(k):
            n = CONV * QKV + SCONV * KD + k
            return cols[:, n:n + 1]

        mixer = ctx.enter_context(ExitStack())

        def mix_sb(name, shape, dt=F32):
            return mixer.enter_context(nc.sbuf_tensor(name, shape, dt))

        xT_hi = mix_sb("xT_hi", [P, KD, SEQ], F32R)
        xT_lo = mix_sb("xT_lo", [P, KD, SEQ], F32R)
        ybT = mix_sb("ybT", [P, KD, SEQ])

        front = ctx.enter_context(ExitStack())

        def front_sb(name, shape, dt=F32):
            return front.enter_context(nc.sbuf_tensor(name, shape, dt))

        qkvT = front_sb("qkvT", [P, QKV, SEQ])
        p1 = ExitStack()

        def p1_sb(name, shape, dt=F32):
            return p1.enter_context(nc.sbuf_tensor(name, shape, dt))

        raw = p1_sb("raw", [P, 2, GT, GW])
        hi = p1_sb("hi", [P, 2, GT, GW], F32R)
        lo = p1_sb("lo", [P, 2, GT, GW], F32R)
        wab_hi = p1_sb("wab_hi", [P, KD, P], F32R)
        wab_lo = p1_sb("wab_lo", [P, KD, P], F32R)
        gbT = p1_sb("gbT", [P, GT, SEQ])
        acc = p1_sb("acc", [P, 2, SEQ])
        mprod = p1_sb("mprod", [P, 1, SEQ])
        stat = p1_sb("stat", [P, 3, TT])
        x_rows = qkvT[:, 0:8, :].rearrange("p a b -> p (a b)").rearrange("p (t d) -> p t d", t=TT)
        squares = qkvT[:, 8:16, :].rearrange("p a b -> p (a b)").rearrange("p (t d) -> p t d", t=TT)
        small_rows = qkvT[:, 16, 0:P]
        wab_raw = qkvT[:, 18:20, :].rearrange("p a b -> p (a b)").rearrange("p (k c) -> p k c", k=KD)
        level_mask = qkvT[:, 20:22, :].rearrange("p a b -> p (a b)").rearrange("p (l c) -> p l c", l=8)

        FIRST_COL = [XS0, GB0, GC0, XS0 + GW, GB0 + GW, GC0 + GW, Z0, Z0 + GW]
        FLAT = len(FIRST_COL)
        QKV_GROUPS = QKV // GT

        s_rows = mixer_sem("s_rows_loaded")
        s_const = mixer_sem("s_constants_loaded")
        s_ab_raw = mixer_sem("s_ab_weights_loaded")
        s_x = [mixer_sem(f"s_x_loaded{t}") for t in range(TT)]
        s_raw = [mixer_sem(f"s_raw_loaded{k}") for k in range(2)]
        s_h = mixer_sem("s_hi_ready")
        s_l = mixer_sem("s_lo_ready")
        s_used = mixer_sem("s_chunk_used")
        s_grp = mixer_sem("s_group_done")
        s_bank = [mixer_sem(f"s_banks_read{k}") for k in range(2)]
        s_k = mixer_sem("s_masks")
        s_ab_zero = mixer_sem("s_ab_weights_zeroed")
        s_sq = mixer_sem("s_squares_summed")
        s_var = mixer_sem("s_variance_ready")
        s_std = mixer_sem("s_std_ready")
        s_xs = mixer_sem("s_x_scaled")
        s_colT = mixer_sem("s_cols_turned")
        s_col = mixer_sem("s_cols_ready")
        s_xT = mixer_sem("s_x_turned")
        s_xh = mixer_sem("s_xT_hi_ready")
        s_xl = mixer_sem("s_xT_lo_ready")
        s_yb = mixer_sem("s_yb_ready")
        s_silu = mixer_sem("s_silu_done")
        s_z = mixer_sem("s_z_ready")
        s_abh = mixer_sem("s_ab_hi_ready")
        s_abl = mixer_sem("s_ab_lo_ready")
        s_abp = mixer_sem("s_ab_projected")
        s_ab = mixer_sem("s_ab_ready")
        s_v = mixer_sem("s_vector_step")

        p1_psum = ExitStack()
        PS = p1_psum.enter_context(nc.psum_tensor("PS", [P, 2 * GT, GW], F32))
        w_in_k = w_in_d.rearrange("(k p) c -> p k c", p=P)

        with nc.Block() as block:
            @block.sync
            def _(sp):
                n = 0
                for src, rows in ((gdn_conv_w[0].rearrange("j (c p) -> (j c) p", p=P), CONV * QKV),
                                  (sconv_w[0].rearrange("j (c p) -> (j c) p", p=P), SCONV * KD),
                                  (norm_mix_g[0].rearrange("(c p) -> c p", p=P), KD)):
                    sp.dma_start(small_rows[n:n + rows, :], src).then_inc(s_rows, 16)
                    n += rows
                for t in range(TT):
                    sp.dma_start(x_rows[:, t, :], x_d[:, t, :]).then_inc(s_x[t], 16)

                def load(g, column):
                    for kq in range(2):
                        wait(sp, s_l, 2 * g + kq - 1)
                        src = w_in_k[:, kq * GT:(kq + 1) * GT, bass.ds(column, GW)]
                        sp.dma_start(raw[:, kq, :, :], src).then_inc(s_raw[kq], 16)

                load(0, FIRST_COL[0])
                sp.wait_ge(s_ab_zero, 1)
                for first, part in ((A0, 0), (B0, 32)):
                    sp.dma_start(wab_raw[:, :, part:part + HEADS],
                                 w_in_k[:, :, first:first + HEADS]).then_inc(s_ab_raw, 16)
                sp.dma_start(gdn_gain[:, :], col(gdn_norm_g[0])).then_inc(s_const, 16)
                sp.dma_start(decay_rate[0:HEADS, :], col(gdn_A_log[0])).then_inc(s_const, 16)
                sp.dma_start(dt_bias[0:HEADS, :], col(gdn_dt_bias[0])).then_inc(s_const, 16)
                for g in range(1, FLAT):
                    load(g, FIRST_COL[g])
                with sp.Fori(0, QKV_GROUPS) as q:
                    load(q + FLAT, q * GW)

            @block.gpsimd
            def _(pool):
                for tile, value in ((ident, 0.0), (tri, 1.0), (strict, 1.0), (level_mask, 1.0)):
                    nc.gpsimd.memset(tile[:], value).then_inc(s_k, 1)
                nc.gpsimd.memset(wab_raw[:], 0.0).then_inc(s_ab_zero, 1)
                pool.wait_ge(s_k, 4)
                nc.gpsimd.affine_select(out=ident[:], in_=ident[:], compare_op=ALU.not_equal, fill=1.0, base=0,
                                        pattern=[[-1, P]], channel_multiplier=1).then_inc(s_k, 1)
                nc.gpsimd.affine_select(out=tri[:], in_=tri[:], compare_op=ALU.is_ge, fill=0.0, base=0,
                                        pattern=[[1, P]], channel_multiplier=-1).then_inc(s_k, 1)
                nc.gpsimd.affine_select(out=strict[:], in_=strict[:], compare_op=ALU.is_gt, fill=0.0, base=0,
                                        pattern=[[1, P]], channel_multiplier=-1).then_inc(s_k, 1)
                for lv in range(LEVELS):
                    n = 1 << lv
                    block_of = level_mask[:, lv, :].rearrange("p (b r) -> p b r", r=n)
                    nc.gpsimd.affine_select(out=block_of, in_=block_of, compare_op=ALU.is_ge, fill=0.0, base=0,
                                            pattern=[[-n, P // n], [0, n]], channel_multiplier=1).then_inc(s_k, 1)
                    pool.wait_ge(s_k, 8 + 2 * lv)
                    nc.gpsimd.affine_select(out=block_of, in_=block_of, compare_op=ALU.is_ge, fill=0.0, base=n - 1,
                                            pattern=[[n, P // n], [0, n]], channel_multiplier=-1).then_inc(s_k, 1)
                pool.wait_ge(s_k, 7 + 2 * LEVELS)
                nc.gpsimd.tensor_tensor(pair_mask[:], level_mask[:, 1:8, :], level_mask[:, 0:7, :],
                                        ALU.subtract).then_inc(s_k, 1)

            @block.scalar
            def _(act):
                for t in range(TT):
                    act.wait_ge(s_x[t], 16)
                    nc.scalar.activation(squares[:, t, :], x_rows[:, t, :], ACT.Square,
                                         accum_out=stat[:, 0, t:t + 1]).then_inc(s_sq, 1)
                act.wait_ge(s_var, 1)
                nc.scalar.activation(stat[:, 2, :], stat[:, 1, :], ACT.Sqrt).then_inc(s_std, 1)
                act.wait_ge(s_col, 1)
                for k in range(KD):
                    act.wait_ge(s_xT, k + 1)
                    nc.scalar.activation(xT_hi[:, k, :], PS[:, k, :], ACT.Copy, scale=mix_gain(k)).then_inc(s_xh, 1)

                def split(g):
                    for kq in range(2):
                        act.wait_ge(s_raw[kq], 16 * (g + 1))
                        wait(act, s_grp if kq else s_used, g)
                        nc.scalar.activation(hi[:, kq, :, :], raw[:, kq, :, :], ACT.Copy).then_inc(s_h, 1)

                split(0)
                act.wait_ge(s_ab_raw, 32)
                nc.scalar.activation(wab_hi[:], wab_raw[:], ACT.Copy).then_inc(s_abh, 1)
                for g in range(FLAT):
                    split(g + 1)
                    if g in (2, 5):
                        continue
                    act.wait_ge(s_grp, g + 1)
                    if g == 4:
                        act.wait_ge(s_yb, GT)
                    for j in range(GT):
                        if g in (0, 3):
                            dst, func = ybT[:, GT * (g // 3) + j, :], ACT.Copy
                        elif g in (1, 4):
                            dst, func = gbT[:, j, :], ACT.Copy
                        else:
                            dst, func = zT[:, GT * (g - 6) + j, :], ACT.Silu
                        nc.scalar.activation(dst, PS[:, GT * (g % 2) + j, :], func).then_inc(s_bank[g % 2], 1)
                act.wait_ge(s_abp, 1)
                nc.scalar.activation(ab[:, :], PS[:, 0, :], ACT.Copy).then_inc(s_ab, 1)
                act.wait_ge(s_k, 8 + 2 * LEVELS)
                act.sem_inc(s_silu, 2)

                def silu(q, s, groups_before):
                    for j in range(GT):
                        act.wait_ge(s_bank[s], GT * (groups_before + q) + j + 1)
                        nc.scalar.activation(qkvT[:, bass.ds(GT * (2 * q + s) + j, 1), :].rearrange("p a t -> p (a t)"),
                                             acc[:, j % 2, :], ACT.Silu).then_inc(s_silu, 1)

                def pair(q, last):
                    split(2 * q + FLAT + 1)
                    silu(q, 0, FLAT // 2)
                    if not last:
                        split(2 * q + FLAT + 2)
                    silu(q, 1, FLAT // 2)

                with act.Fori(0, QKV_GROUPS // 2 - 1) as q:
                    pair(q, False)
                pair(QKV_GROUPS // 2 - 1, True)

            @block.vector
            def _(dve):
                steps = [0]

                def link(ins):
                    steps[0] = steps[0] + 1
                    ins.then_inc(s_v, 1)
                    dve.wait_ge(s_v, steps[0])

                dve.wait_ge(s_sq, TT)
                nc.vector.tensor_scalar(stat[:, 1, :], stat[:, 0, :], 1.0 / D, EPS, ALU.mult, ALU.add).then_inc(s_var, 1)
                dve.wait_ge(s_std, 1)
                link(nc.vector.reciprocal(stat[:, 0, :], stat[:, 2, :]))
                for t in range(TT):
                    nc.vector.tensor_scalar(x_rows[:, t, :], x_rows[:, t, :], stat[:, 0, t:t + 1], None,
                                            ALU.mult).then_inc(s_xs, 1)
                dve.wait_ge(s_colT, 1)
                nc.vector.tensor_copy(cols[:, :], PS[:, 7, 0:P]).then_inc(s_col, 1)
                dve.wait_ge(s_col, 1)
                for k in range(KD):
                    dve.wait_ge(s_xh, k + 1)
                    nc.vector.scalar_tensor_tensor(out=xT_lo[:, k, :], in0=PS[:, k, :], scalar=mix_gain(k),
                                                   in1=xT_hi[:, k, :].bitcast(F32), op0=ALU.mult,
                                                   op1=ALU.subtract).then_inc(s_xl, 1)

                def split(g):
                    for kq in range(2):
                        dve.wait_ge(s_h, 2 * g + kq + 1)
                        nc.vector.tensor_tensor(lo[:, kq, :, :], raw[:, kq, :, :], hi[:, kq, :, :].bitcast(F32),
                                                ALU.subtract).then_inc(s_l, 1)

                split(0)
                dve.wait_ge(s_abh, 1)
                nc.vector.tensor_tensor(wab_lo[:], wab_raw[:], wab_hi[:].bitcast(F32), ALU.subtract).then_inc(s_abl, 1)
                for g in range(FLAT):
                    split(g + 1)
                    if g in (2, 5):
                        dve.wait_ge(s_grp, g + 1)
                        dve.wait_ge(s_bank[0], GT * (1 if g == 2 else 3))
                        dve.wait_ge(s_bank[1], GT * (1 if g == 2 else 2))
                        for j in range(GT):
                            c = GT * (g // 3) + j
                            m, a = mprod[:, 0, :], acc[:, 0, :]
                            nc.vector.tensor_tensor(m, PS[:, GT * (g % 2) + j, :], ybT[:, c, :],
                                                    ALU.mult).then_inc(s_bank[g % 2], 1)
                            dve.wait_ge(s_bank[g % 2], GT * (g // 2) + j + 1)
                            link(nc.vector.tensor_scalar(a, m, sconv_tap(SCONV - 1, c), None, ALU.mult))
                            for s in range(1, SCONV):
                                link(nc.vector.scalar_tensor_tensor(
                                    out=a[:, s:], in0=m[:, :SEQ - s], scalar=sconv_tap(SCONV - 1 - s, c),
                                    in1=a[:, s:], op0=ALU.mult, op1=ALU.add))
                            nc.vector.tensor_tensor(ybT[:, c, :], a, gbT[:, j, :], ALU.mult).then_inc(s_yb, 1)
                            dve.wait_ge(s_yb, c + 1)
                    if g >= 6:
                        dve.wait_ge(s_const, 48)
                        for j in range(GT):
                            dve.wait_ge(s_bank[g % 2], GT * (g // 2) + j + 1)
                            c = GT * (g - 6) + j
                            nc.vector.tensor_scalar(zT[:, c, :], zT[:, c, :], gdn_gain[:, 0:1], None,
                                                    ALU.mult).then_inc(s_z, 1)

                def conv(q, s, groups_before):
                    dve.wait_ge(s_grp, 2 * q + FLAT + s + 1)
                    for j in range(GT):
                        tile = GT * (2 * q + s) + j
                        dve.wait_ge(s_silu, tile + 1)
                        a, src = acc[:, j % 2, :], PS[:, GT * s + j, :]
                        first = steps[0] + (CONV - 1) * (GT * (2 * q + s) + j)
                        nc.vector.tensor_scalar(a, src, tap_of(CONV - 1, tile), None, ALU.mult).then_inc(s_v, 1)
                        for d in range(1, CONV):
                            dve.wait_ge(s_v, first + d)
                            ins = nc.vector.scalar_tensor_tensor(
                                out=a[:, d:], in0=src[:, :SEQ - d], scalar=tap_of(CONV - 1 - d, tile),
                                in1=a[:, d:], op0=ALU.mult, op1=ALU.add)
                            ins.then_inc(s_v if d < CONV - 1 else s_bank[s], 1)

                def tap_of(j, tile):
                    return cols[:, bass.ds(tile + j * QKV, 1)]

                def pair(q, last):
                    split(2 * q + FLAT + 1)
                    conv(q, 0, FLAT // 2)
                    if not last:
                        split(2 * q + FLAT + 2)
                    conv(q, 1, FLAT // 2)

                with dve.Fori(0, QKV_GROUPS // 2 - 1) as q:
                    pair(q, False)
                pair(QKV_GROUPS // 2 - 1, True)

            @block.tensor
            def _(pe):
                pe.wait_ge(s_k, 5)
                pe.wait_ge(s_rows, 48)
                pe.transpose(PS[:, 7, 0:P], small_rows[:, :], ident[:, :]).then_inc(s_colT, 1)
                pe.wait_ge(s_xs, TT)
                for k in range(KD):
                    if k == KD - 1:
                        pe.wait_ge(s_col, 1)
                    for t in range(TT):
                        mm = pe.transpose(PS[:, k, t * P:(t + 1) * P], x_rows[:, t, k * P:(k + 1) * P], ident[:, :])
                    mm.then_inc(s_xT, 1)
                pe.wait_ge(s_xl, KD)

                def group(g, s):
                    for kq in range(2):
                        pe.wait_ge(s_l, 2 * g + kq + 1)
                        for kk in range(GT):
                            k = GT * kq + kk
                            for j in range(GT):
                                w_hi, w_lo = hi[:, kq, kk, j * P:(j + 1) * P], lo[:, kq, kk, j * P:(j + 1) * P]
                                dst = PS[:, GT * s + j, :]
                                pe.matmul(dst, w_hi, xT_hi[:, k, :], start=(k == 0), stop=False)
                                pe.matmul(dst, w_hi, xT_lo[:, k, :], start=False, stop=False)
                                mm = pe.matmul(dst, w_lo, xT_hi[:, k, :], start=False, stop=(k == KD - 1))
                                if k == KD - 1 and j == GT - 1:
                                    mm.then_inc(s_grp, 1)
                                elif kk == GT - 1 and j == GT - 1:
                                    mm.then_inc(s_used, 1)

                for g in range(FLAT):
                    wait(pe, s_bank[g % 2], GT * (g // 2))
                    group(g, g % 2)
                pe.wait_ge(s_bank[0], GT * (FLAT // 2))
                pe.wait_ge(s_abl, 1)
                for k in range(KD):
                    pe.matmul(PS[:, 0, :], wab_hi[:, k, :], xT_hi[:, k, :], start=(k == 0), stop=False)
                    pe.matmul(PS[:, 0, :], wab_hi[:, k, :], xT_lo[:, k, :], start=False, stop=False)
                    mm = pe.matmul(PS[:, 0, :], wab_lo[:, k, :], xT_hi[:, k, :], start=False, stop=(k == KD - 1))
                mm.then_inc(s_abp, 1)
                pe.wait_ge(s_ab, 1)
                with pe.Fori(0, QKV_GROUPS // 2) as q:
                    for s in range(2):
                        pe.wait_ge(s_bank[s], GT * (FLAT // 2) + GT * q)
                        group(2 * q + FLAT + s, s)
        p1_psum.close()
        p1.close()
        HS = HEADS // 2
        BOTH = range(2)
        p2 = ExitStack()

        def p2_sb(name, shape, dt=F32):
            return p2.enter_context(nc.sbuf_tensor(name, shape, dt))

        stage = p2_sb("stage", [P, QKV, P])
        qn = p2_sb("qn", [P, HEADS, P])
        kn = p2_sb("kn", [P, HEADS, P])
        kb = p2_sb("kb", [P, HEADS, P])
        kd = p2_sb("kd", [P, HEADS, P])
        vb = p2_sb("vb", [P, HEADS, P])
        qT = p2_sb("qT", [P, HEADS, P])
        kT = p2_sb("kT", [P, HEADS, P])
        kbT = p2_sb("kbT", [P, HEADS, P])
        dec = p2_sb("dec", [P, HEADS, P])
        decs = p2_sb("decs", [P, HEADS, P])
        LT = p2_sb("LT", [P, HEADS, P])
        aqkT = p2_sb("aqkT", [P, HEADS, P])
        T = p2_sb("T", [P, HEADS, P])
        U = p2_sb("U", [P, HEADS, P])
        state = p2_sb("state", [P, HEADS, P])
        gtok = p2_sb("gtok", [P, TT, HEADS])
        btok = p2_sb("btok", [P, TT, HEADS])
        norms = p2_sb("norms", [P, 4, 2 * HEADS])
        gates = p2_sb("gates", [P, 8, HEADS])
        gbc, Y = T, kb
        sp_s, sp_e, sp_n = (t[:, 0:HS, :].rearrange("p a t -> p (a t)") for t in (LT, aqkT, U))
        MT = (qn, kn)
        q_state, r, vnew, o = kbT, dec, decs, kb
        sq = (LT, aqkT)
        gc, eg, egl, ekd, eb = (gates[:, n, :] for n in range(5))
        o_norm = gates[:, 5:8, :]

        def heads(tile, g):
            return tile[:, HS * g:HS * (g + 1), :]

        def wide(small):
            return small.unsqueeze(2).to_broadcast([P, small.shape[1], P])

        def each(mask):
            return mask.unsqueeze(1).to_broadcast([P, HS, P])

        s_beta = mixer_sem("s_beta_ready")
        s_g1 = mixer_sem("s_decay_act")
        s_gv = mixer_sem("s_decay_vector")
        s_gready = mixer_sem("s_decay_ready")
        s_tokT = mixer_sem("s_gates_turned")
        s_tok = mixer_sem("s_gates_by_token")
        s_stage = mixer_sem("s_stage_loaded")
        s_tq, s_tk, s_tv = mixer_sem("s_q_turned"), mixer_sem("s_k_turned"), mixer_sem("s_v_turned")
        s_sqr, s_red, s_pow, s_powin = mixer_sem("s_qk_squared"), mixer_sem("s_qk_summed"), mixer_sem("s_qk_norms"), mixer_sem("s_qk_norms_asked")
        s_gbc, s_gcum, s_gcb = mixer_sem("s_g_spread"), mixer_sem("s_gcum"), mixer_sem("s_gcum_rows")
        s_gc, s_diff, s_exp = mixer_sem("s_gcum_copied"), mixer_sem("s_decay_diff"), mixer_sem("s_decay_exp")
        s_small, s_sexp, s_eb = mixer_sem("s_last_diff"), mixer_sem("s_small_exps"), mixer_sem("s_beta_decay")
        s_dect, s_decs = mixer_sem("s_decay_causal"), mixer_sem("s_decay_strict")
        s_vb, s_qn, s_kn, s_kb, s_kd = mixer_sem("s_vb"), mixer_sem("s_qn"), mixer_sem("s_kn"), mixer_sem("s_kb"), mixer_sem("s_kd")
        s_bq, s_bk, s_bkb = mixer_sem("s_q_back"), mixer_sem("s_k_back"), mixer_sem("s_kb_back")
        s_qT, s_kT, s_kbT = mixer_sem("s_qT"), mixer_sem("s_kT"), mixer_sem("s_kbT")
        s_G, s_A = mixer_sem("s_kk_products"), mixer_sem("s_qk_products")
        s_LT, s_AT = mixer_sem("s_LT"), mixer_sem("s_aqkT")
        s_MT = mixer_sem("s_level_mask")
        s_U, s_UT, s_T = mixer_sem("s_U"), mixer_sem("s_U_turned"), mixer_sem("s_T")
        s_Yp, s_Y, s_PT = mixer_sem("s_Y_product"), mixer_sem("s_Y"), mixer_sem("s_PT_product")
        s_kS, s_r1, s_r, s_qS, s_oS = mixer_sem("s_k_state"), mixer_sem("s_r_part"), mixer_sem("s_r"), mixer_sem("s_q_state"), mixer_sem("s_o_state")
        s_vn, s_vnew, s_oa, s_o = mixer_sem("s_v_new_product"), mixer_sem("s_v_new"), mixer_sem("s_o_product"), mixer_sem("s_o")
        s_Sd, s_Sp, s_S = mixer_sem("s_state_decayed"), mixer_sem("s_state_product"), mixer_sem("s_state")
        s_osq, s_ored, s_opin, s_opow, s_on = (mixer_sem("s_o_squared"), mixer_sem("s_o_summed"), mixer_sem("s_o_norm_asked"),
                                               mixer_sem("s_o_norm"), mixer_sem("s_o_scaled"))
        s_oT, s_chunk = mixer_sem("s_o_turned"), mixer_sem("s_chunk_done")
        s_half = mixer_sem("s_minus_half")
        s_v2, s_v3, s_v4 = mixer_sem("s_vector_decays"), mixer_sem("s_vector_norms"), mixer_sem("s_vector_gated")

        p2_psum = ExitStack()
        PB = p2_psum.enter_context(nc.psum_tensor("PB", [P, 8, HS, P], F32))
        minus_half = p2_sb("minus_half", [P, 2 * HEADS])

        with nc.Block() as block:
            @block.sync
            def _(sp):
                sp.dma_start(stage[:], qkvT[:, :, 0:P]).then_inc(s_stage, 16)
                with sp.Fori(1, TT) as c:
                    sp.wait_ge(s_tv, 2 * c)
                    sp.dma_start(stage[:], qkvT[:, :, bass.ds(c * P, P)]).then_inc(s_stage, 16)

            @block.gpsimd
            def _(pool):
                nc.gpsimd.memset(minus_half[:], -0.5).then_inc(s_half, 1)
                pool.wait_ge(s_half, 1)
                with pool.Fori(0, TT) as c:
                    pool.wait_ge(s_powin, c + 1)
                    nc.gpsimd.tensor_tensor(norms[:, 2, :], norms[:, 1, :], minus_half[:], ALU.pow).then_inc(s_pow, 1)
                    for g in BOTH:
                        pool.wait_ge(s_exp, 2 * c + g + 1)
                        nc.gpsimd.tensor_tensor(heads(decs, g), heads(dec, g), each(strict[:]), ALU.mult).then_inc(s_decs, 1)
                        pool.wait_ge(s_decs, 2 * c + g + 1)
                        nc.gpsimd.tensor_tensor(heads(dec, g), heads(dec, g), each(tri[:]), ALU.mult).then_inc(s_dect, 1)
                    for g in BOTH:
                        pool.wait_ge(s_kn, 2 * c + g + 1)
                        pool.wait_ge(s_sexp, 3 * c + 3)
                        nc.gpsimd.tensor_tensor(heads(kd, g), heads(kn, g), wide(ekd[:, HS * g:HS * (g + 1)]),
                                                ALU.mult).then_inc(s_kd, 1)
                    for lv in range(LEVELS):
                        for g in BOTH:
                            if lv == 0:
                                pool.wait_ge(s_LT, 2 * c + g + 1)
                                pool.wait_ge(s_qT, 2 * c + g + 1)
                            if lv == 1:
                                pool.wait_ge(s_kT, 2 * c + g + 1)
                                pool.wait_ge(s_kd, 2 * c + g + 1)
                            if lv == 2:
                                pool.wait_ge(s_U, 2 * LEVELS * c + g + 1)
                            if lv >= 3:
                                pool.wait_ge(s_Yp, 2 * (LEVELS - 1) * c + 2 * (lv - 3) + g + 1)
                            nc.gpsimd.tensor_tensor(heads(MT[lv % 2], g), heads(LT, g), each(pair_mask[:, lv, :]),
                                                    ALU.mult).then_inc(s_MT, 1)
                    for g in BOTH:
                        pool.wait_ge(s_r1, 2 * c + g + 1)
                        pool.wait_ge(s_oS, 2 * c + g + 1)
                        nc.gpsimd.tensor_tensor(heads(state, g), heads(state, g), wide(egl[:, HS * g:HS * (g + 1)]),
                                                ALU.mult).then_inc(s_Sd, 1)
                    pool.wait_ge(s_opin, c + 1)
                    nc.gpsimd.tensor_tensor(o_norm[:, 2, :], o_norm[:, 1, :], minus_half[:, 0:HEADS],
                                            ALU.pow).then_inc(s_opow, 1)

            @block.scalar
            def _(act):
                nc.scalar.activation(ab[32:32 + HEADS, :], ab[32:32 + HEADS, :], ACT.Sigmoid).then_inc(s_beta, 1)
                nc.scalar.activation(decay_rate[0:HEADS, :], decay_rate[0:HEADS, :], ACT.Exp).then_inc(s_g1, 1)
                act.wait_ge(s_gv, 3)
                nc.scalar.activation(sp_e[0:HEADS, :], sp_n[0:HEADS, :], ACT.Exp).then_inc(s_g1, 1)
                act.wait_ge(s_gv, 4)
                nc.scalar.activation(sp_n[0:HEADS, :], sp_e[0:HEADS, :], ACT.Ln).then_inc(s_g1, 1)

                with act.Fori(0, TT) as c:
                    for n, turned in ((0, s_tq), (2, s_tk)):
                        for g in BOTH:
                            act.wait_ge(turned, 2 * c + g + 1)
                            nc.scalar.activation(heads(sq[n // 2], g), PB[:, n + g], ACT.Square).then_inc(s_sqr, 1)
                    for g in BOTH:
                        act.wait_ge(s_diff, 2 * c + g + 1)
                        nc.scalar.activation(heads(dec, g), heads(dec, g), ACT.Exp).then_inc(s_exp, 1)
                    act.wait_ge(s_gc, c + 1)
                    nc.scalar.activation(eg, gc, ACT.Exp).then_inc(s_sexp, 1)
                    act.wait_ge(s_small, 2 * c + 2)
                    nc.scalar.activation(egl, egl, ACT.Exp).then_inc(s_sexp, 1)
                    nc.scalar.activation(ekd, ekd, ACT.Exp).then_inc(s_sexp, 1)
                    for bank, src, dst, done in ((0, s_bq, qT, s_qT), (2, s_bk, kT, s_kT)):
                        for g in BOTH:
                            act.wait_ge(src, 2 * c + g + 1)
                            nc.scalar.activation(heads(dst, g), PB[:, bank + g], ACT.Copy).then_inc(done, 1)
                    for g in BOTH:
                        act.wait_ge(s_UT, 2 * (LEVELS - 1) * c + g + 1)
                        nc.scalar.activation(heads(T, g), PB[:, 4 + g], ACT.Copy).then_inc(s_T, 1)
                    for lv in range(1, LEVELS):
                        for g in BOTH:
                            act.wait_ge(s_Yp, 2 * (LEVELS - 1) * c + 2 * (lv - 1) + g + 1)
                            nc.scalar.activation(heads(Y, g), PB[:, g], ACT.Copy).then_inc(s_Y, 1)
                        if lv < LEVELS - 1:
                            for g in BOTH:
                                act.wait_ge(s_UT, 2 * (LEVELS - 1) * c + 2 * lv + g + 1)
                                nc.scalar.activation(heads(T, g), PB[:, 4 + g], ACT.Copy).then_inc(s_T, 1)
                    for g in BOTH:
                        act.wait_ge(s_vn, 2 * c + g + 1)
                        nc.scalar.activation(heads(vnew, g), PB[:, g], ACT.Copy).then_inc(s_vnew, 1)
                    for g in BOTH:
                        act.wait_ge(s_o, 2 * c + g + 1)
                        nc.scalar.activation(heads(sq[0], g), heads(o, g), ACT.Square).then_inc(s_osq, 1)

            @block.vector
            def _(dve):
                a = ab[0:HEADS, :]
                nc.vector.tensor_scalar(sp_s[0:HEADS, :], a, dt_bias[0:HEADS, 0:1], None, ALU.add).then_inc(s_gv, 1)
                dve.wait_ge(s_gv, 1)
                nc.vector.tensor_scalar(sp_e[0:HEADS, :], sp_s[0:HEADS, :], -1.0, None, ALU.mult).then_inc(s_gv, 1)
                dve.wait_ge(s_gv, 2)
                nc.vector.tensor_tensor(sp_n[0:HEADS, :], sp_s[0:HEADS, :], sp_e[0:HEADS, :], ALU.min).then_inc(s_gv, 1)
                dve.wait_ge(s_g1, 2)
                nc.vector.tensor_scalar(sp_e[0:HEADS, :], sp_e[0:HEADS, :], 1.0, None, ALU.add).then_inc(s_gv, 1)
                dve.wait_ge(s_g1, 3)
                nc.vector.scalar_tensor_tensor(out=sp_s[0:HEADS, :], in0=sp_s[0:HEADS, :], scalar=0.0,
                                               in1=sp_n[0:HEADS, :], op0=ALU.max, op1=ALU.add).then_inc(s_gv, 1)
                dve.wait_ge(s_gv, 5)
                nc.vector.tensor_scalar(a, sp_s[0:HEADS, :], decay_rate[0:HEADS, 0:1], -1.0, ALU.mult,
                                        ALU.mult).then_inc(s_gready, 1)
                dve.wait_ge(s_tokT, 1)
                turned = PB[:, 0].rearrange("p (t h) c -> p t (h c)", t=TT)
                nc.vector.tensor_copy(gtok[:], turned[:, :, 0:HEADS]).then_inc(s_tok, 1)
                nc.vector.tensor_copy(btok[:], turned[:, :, 32:32 + HEADS]).then_inc(s_tok, 1)
                dve.wait_ge(s_tok, 2)
                nc.vector.memset(state[:], 0.0).then_inc(s_S, 2)
                nc.vector.memset(gates[:], 0.0).then_inc(s_chunk, 1)

                with dve.Fori(0, TT) as c:
                    g_c = gtok[:, bass.ds(c, 1), :].rearrange("p a h -> p (a h)")
                    b_c = btok[:, bass.ds(c, 1), :].rearrange("p a h -> p (a h)")
                    nc.vector.tensor_copy(gbc[:], wide(g_c)).then_inc(s_gbc, 1)
                    dve.wait_ge(s_gcum, c + 1)
                    nc.vector.tensor_copy(gc, PB[:, 4, 0, 0:HEADS]).then_inc(s_gc, 1)
                    dve.wait_ge(s_gc, c + 1)
                    for g in BOTH:
                        dve.wait_ge(s_gcb, 2 * c + g + 1)
                        hs = slice(HS * g, HS * (g + 1))
                        nc.vector.tensor_tensor(heads(dec, g), PB[:, 6 + g], wide(gc[:, hs]), ALU.subtract).then_inc(s_v2, 1)
                        last = PB[:, 6 + g, :, P - 1]
                        nc.vector.tensor_copy(egl[:, hs], last).then_inc(s_v2, 1)
                        nc.vector.tensor_tensor(ekd[:, hs], last, gc[:, hs], ALU.subtract).then_inc(s_small, 1)
                        dve.wait_ge(s_v2, 4 * c + 2 * g + 2)
                        nc.vector.tensor_scalar(heads(dec, g), heads(dec, g), 0.0, None, ALU.min).then_inc(s_diff, 1)
                    for n in range(2):
                        for g in BOTH:
                            dve.wait_ge(s_sqr, 4 * c + 2 * n + g + 1)
                            nc.vector.tensor_reduce(norms[:, 0, HEADS * n + HS * g:HEADS * n + HS * (g + 1)],
                                                    heads(sq[n], g), AX, ALU.add).then_inc(s_red, 1)
                    dve.wait_ge(s_red, 4 * c + 4)
                    nc.vector.tensor_scalar(norms[:, 1, 0:HEADS], norms[:, 0, 0:HEADS], EPS, float(P), ALU.add,
                                            ALU.mult).then_inc(s_v3, 1)
                    dve.wait_ge(s_v3, c + 1)
                    nc.vector.tensor_scalar(norms[:, 1, HEADS:], norms[:, 0, HEADS:], EPS, None,
                                            ALU.add).then_inc(s_powin, 1)
                    for g in BOTH:
                        dve.wait_ge(s_tv, 2 * c + g + 1)
                        nc.vector.tensor_tensor(heads(vb, g), PB[:, 4 + g], wide(b_c[:, HS * g:HS * (g + 1)]),
                                                ALU.mult).then_inc(s_vb, 1)
                    dve.wait_ge(s_sexp, 3 * c + 3)
                    nc.vector.tensor_tensor(eb, eg, b_c, ALU.mult).then_inc(s_eb, 1)
                    dve.wait_ge(s_pow, c + 1)
                    for g in BOTH:
                        hs = slice(HS * g, HS * (g + 1))
                        nc.vector.tensor_tensor(heads(kn, g), PB[:, 2 + g],
                                                wide(norms[:, 2, HEADS + HS * g:HEADS + HS * (g + 1)]),
                                                ALU.mult).then_inc(s_kn, 1)
                        nc.vector.tensor_tensor(heads(qn, g), PB[:, g], wide(norms[:, 2, hs]), ALU.mult).then_inc(s_qn, 1)
                        dve.wait_ge(s_kn, 2 * c + g + 1)
                        nc.vector.tensor_tensor(heads(kb, g), heads(kn, g), wide(b_c[:, hs]), ALU.mult).then_inc(s_kb, 1)
                    for g in BOTH:
                        dve.wait_ge(s_bkb, 2 * c + g + 1)
                        nc.vector.tensor_copy(heads(kbT, g), PB[:, 4 + g]).then_inc(s_kbT, 1)
                    for g in BOTH:
                        dve.wait_ge(s_G, 2 * c + g + 1)
                        dve.wait_ge(s_decs, 2 * c + g + 1)
                        nc.vector.tensor_tensor(heads(LT, g), PB[:, g], heads(decs, g), ALU.mult).then_inc(s_LT, 1)
                    for g in BOTH:
                        dve.wait_ge(s_A, 2 * c + g + 1)
                        dve.wait_ge(s_dect, 2 * c + g + 1)
                        nc.vector.tensor_tensor(heads(aqkT, g), PB[:, 2 + g], heads(dec, g), ALU.mult).then_inc(s_AT, 1)
                    for g in BOTH:
                        dve.wait_ge(s_MT, 2 * LEVELS * c + g + 1)
                        nc.vector.tensor_tensor(heads(U, g), each(ident[:]), heads(MT[0], g), ALU.subtract).then_inc(s_U, 1)

                    def with_old_state():
                        for g in BOTH:
                            hs = slice(HS * g, HS * (g + 1))
                            dve.wait_ge(s_kS, 2 * c + g + 1)
                            dve.wait_ge(s_eb, c + 1)
                            dve.wait_ge(s_AT, 2 * c + g + 1)
                            nc.vector.tensor_tensor(heads(r, g), PB[:, 6 + g], wide(eb[:, hs]), ALU.mult).then_inc(s_r1, 1)
                            dve.wait_ge(s_r1, 2 * c + g + 1)
                            dve.wait_ge(s_vb, 2 * c + g + 1)
                            nc.vector.tensor_tensor(heads(r, g), heads(vb, g), heads(r, g), ALU.subtract).then_inc(s_r, 1)

                    def with_old_state_q():
                        for g in BOTH:
                            hs = slice(HS * g, HS * (g + 1))
                            dve.wait_ge(s_qS, 2 * c + g + 1)
                            nc.vector.tensor_tensor(heads(q_state, g), PB[:, 6 + g], wide(eg[:, hs]),
                                                    ALU.mult).then_inc(s_oS, 1)

                    for lv in range(1, LEVELS):
                        if lv == 1:
                            with_old_state()
                        if lv == 2:
                            with_old_state_q()
                        for g in BOTH:
                            n = 2 * (LEVELS - 1) * c + 2 * (lv - 1) + g + 1
                            dve.wait_ge(s_PT, n)
                            dve.wait_ge(s_U, 2 * LEVELS * c + 2 * (lv - 1) + g + 1)
                            nc.vector.tensor_tensor(heads(U, g), heads(U, g), PB[:, 2 + g], ALU.subtract).then_inc(s_U, 1)
                    for g in BOTH:
                        dve.wait_ge(s_oa, 2 * c + g + 1)
                        dve.wait_ge(s_oS, 2 * c + g + 1)
                        nc.vector.tensor_tensor(heads(o, g), PB[:, 2 + g], heads(q_state, g), ALU.add).then_inc(s_o, 1)
                    for g in BOTH:
                        dve.wait_ge(s_Sp, 2 * c + g + 1)
                        dve.wait_ge(s_Sd, 2 * c + g + 1)
                        nc.vector.tensor_tensor(heads(state, g), heads(state, g), PB[:, 4 + g], ALU.add).then_inc(s_S, 1)
                    for g in BOTH:
                        dve.wait_ge(s_osq, 2 * c + g + 1)
                        nc.vector.tensor_reduce(o_norm[:, 0, HS * g:HS * (g + 1)], heads(sq[0], g), AX,
                                                ALU.add).then_inc(s_ored, 1)
                    dve.wait_ge(s_ored, 2 * c + 2)
                    nc.vector.tensor_scalar(o_norm[:, 1, :], o_norm[:, 0, :], 1.0 / P, EPS, ALU.mult,
                                            ALU.add).then_inc(s_opin, 1)
                    dve.wait_ge(s_opow, c + 1)
                    for g in BOTH:
                        nc.vector.tensor_tensor(heads(o, g), heads(o, g), wide(o_norm[:, 2, HS * g:HS * (g + 1)]),
                                                ALU.mult).then_inc(s_on, 1)
                    for g in BOTH:
                        dve.wait_ge(s_oT, 2 * c + g + 1)
                        gate = zT[:, HS * g:HS * (g + 1), bass.ds(c * P, P)]
                        ins = nc.vector.tensor_tensor(gate, PB[:, 6 + g], gate, ALU.mult)
                        ins.then_inc(s_chunk, 1) if g == 1 else ins.then_inc(s_v4, 1)

            @block.tensor
            def _(pe):
                pe.wait_ge(s_gready, 1)
                pe.wait_ge(s_beta, 1)
                for t in range(TT):
                    mm = pe.transpose(PB[:, 0, t, :], ab[:, t * P:(t + 1) * P], ident[:, :])
                mm.then_inc(s_tokT, 1)
                pe.wait_ge(s_tok, 2)

                def turn(bank, g, src, first):
                    for h in range(HS):
                        mm = pe.transpose(PB[:, bank + g, h, :], src[:, first + HS * g + h, :], ident[:, :])
                    return mm

                def product(bank, g, lhsT, rhs):
                    for h in range(HS):
                        mm = pe.matmul(PB[:, bank + g, h, :], lhsT[:, HS * g + h, :], rhs[:, HS * g + h, :],
                                       start=True, stop=True)
                    return mm

                with pe.Fori(0, TT) as c:
                    pe.wait_ge(s_chunk, c + 1)
                    pe.wait_ge(s_gbc, c + 1)
                    pe.matmul(PB[:, 4, 0, 0:HEADS], tri[:, :], gtok[:, bass.ds(c, 1), :].rearrange("p a h -> p (a h)"),
                              start=True, stop=True).then_inc(s_gcum, 1)
                    for g in BOTH:
                        for h in range(HS):
                            mm = pe.matmul(PB[:, 6 + g, h, :], gbc[:, HS * g + h, :], tri[:, :], start=True, stop=True)
                        mm.then_inc(s_gcb, 1)
                    pe.wait_ge(s_stage, 16 * (c + 1))
                    for bank, first, done in ((0, 0, s_tq), (2, HEADS, s_tk), (4, 2 * HEADS, s_tv)):
                        if bank == 4:
                            pe.wait_ge(s_gc, c + 1)
                        for g in BOTH:
                            turn(bank, g, stage, first).then_inc(done, 1)
                    for g in BOTH:
                        pe.wait_ge(s_qn, 2 * c + g + 1)
                        turn(0, g, qn, 0).then_inc(s_bq, 1)
                        pe.wait_ge(s_kn, 2 * c + g + 1)
                        turn(2, g, kn, 0).then_inc(s_bk, 1)
                        pe.wait_ge(s_kb, 2 * c + g + 1)
                        pe.wait_ge(s_vb, 2 * c + g + 1)
                        turn(4, g, kb, 0).then_inc(s_bkb, 1)
                    for g in BOTH:
                        pe.wait_ge(s_qT, 2 * c + g + 1)
                        pe.wait_ge(s_kT, 2 * c + g + 1)
                        pe.wait_ge(s_kbT, 2 * c + g + 1)
                        product(0, g, kT, kbT).then_inc(s_G, 1)
                        product(2, g, kT, qT).then_inc(s_A, 1)
                    for g in BOTH:
                        pe.wait_ge(s_diff, 2 * c + g + 1)
                        pe.wait_ge(s_S, 2 * c + g + 1)
                        product(6, g, kT, state).then_inc(s_kS, 1)
                    for g in BOTH:
                        pe.wait_ge(s_U, 2 * LEVELS * c + g + 1)
                        turn(4, g, U, 0).then_inc(s_UT, 1)
                    for lv in range(1, LEVELS):
                        n = 2 * (LEVELS - 1) * c + 2 * (lv - 1)
                        for g in BOTH:
                            pe.wait_ge(s_T, n + g + 1)
                            pe.wait_ge(s_MT, 2 * LEVELS * c + 2 * lv + g + 1)
                            product(0, g, MT[lv % 2], T).then_inc(s_Yp, 1)
                        if lv == 1:
                            for g in BOTH:
                                pe.wait_ge(s_r1, 2 * c + g + 1)
                                product(6, g, qT, state).then_inc(s_qS, 1)
                        for g in BOTH:
                            pe.wait_ge(s_Y, n + g + 1)
                            if lv == 1:
                                pe.wait_ge(s_AT, 2 * c + g + 1)
                            product(2, g, Y, U).then_inc(s_PT, 1)
                        if lv < LEVELS - 1:
                            for g in BOTH:
                                pe.wait_ge(s_U, 2 * LEVELS * c + 2 * lv + g + 1)
                                turn(4, g, U, 0).then_inc(s_UT, 1)
                    for g in BOTH:
                        pe.wait_ge(s_U, 2 * LEVELS * c + 2 * (LEVELS - 1) + g + 1)
                        pe.wait_ge(s_r, 2 * c + g + 1)
                        product(0, g, U, r).then_inc(s_vn, 1)
                    for g in BOTH:
                        pe.wait_ge(s_vnew, 2 * c + g + 1)
                        product(2, g, aqkT, vnew).then_inc(s_oa, 1)
                        pe.wait_ge(s_kd, 2 * c + g + 1)
                        product(4, g, kd, vnew).then_inc(s_Sp, 1)
                    for g in BOTH:
                        pe.wait_ge(s_on, 2 * c + g + 1)
                        turn(6, g, o, 0).then_inc(s_oT, 1)
        p2_psum.close()
        p2.close()
        front.close()
        p3 = ExitStack()

        def p3_sb(name, shape, dt=F32):
            return p3.enter_context(nc.sbuf_tensor(name, shape, dt))

        out_hi = p3_sb("out_hi", [P, KD, SEQ], F32R)
        out_lo = p3_sb("out_lo", [P, KD, SEQ], F32R)
        gateA = p3_sb("gateA", [P, KD, SEQ])
        gateB = p3_sb("gateB", [P, KD, SEQ])
        raw3 = p3_sb("raw3", [P, 2, GT, GW])
        hi3 = p3_sb("hi3", [P, 2, GT, GW], F32R)
        lo3 = p3_sb("lo3", [P, 2, GT, GW], F32R)
        part = p3_sb("part", [P, 2, SEQ])
        h_rows = zT[:].rearrange("p a b -> p (a b)").rearrange("p (t d) -> p t d", t=TT)
        xn2 = gateB[:].rearrange("p a b -> p (a b)").rearrange("p (t d) -> p t d", t=TT)
        xn2T = gateA
        ffn_gain = raw3[:, 0, 0:2, :].rearrange("p a c -> p (a c)")
        router_w = raw3[:, 1, 0, 0:KD * E].rearrange("p (k e) -> p k e", k=KD)
        router_b = raw3[:, 1, 1, 0:E]
        sq3 = ybT[:, 0:2, :].rearrange("p a b -> p (a b)")
        stat3 = ybT[:, 2, 0:16].rearrange("p (n t) -> p n t", n=4)

        def column_source(weights, first):
            return weights.rearrange("(k p) c -> p k c", p=P)[:, :, first:first + GW]

        SOURCES = [column_source(w_in_d, GA0), column_source(w_in_d, GBB0),
                   column_source(w_in_d, GA0 + GW), column_source(w_in_d, GBB0 + GW)]
        for weights in (w_o_gdn[0], w_o_sconv[0], w_mix_out[0]):
            SOURCES += [column_source(weights, 0), column_source(weights, GW)]
        N3 = len(SOURCES)
        GATES, YA, YB, MIX = 0, 4, 6, 8

        t_raw = [sem(f"s_raw3_loaded{k}") for k in range(2)]
        t_h, t_l, t_used, t_grp = sem("s_hi3_ready"), sem("s_lo3_ready"), sem("s_chunk3_used"), sem("s_group3_done")
        t_bank = [sem(f"s_banks3_read{k}") for k in range(2)]
        s_oh, s_ol = sem("s_o_hi"), sem("s_o_lo")
        s_yh, s_yl = sem("s_yb_hi"), sem("s_yb_lo")
        s_part, s_merge, s_mh, s_ml = sem("s_gated_b"), sem("s_merged"), sem("s_merged_hi"), sem("s_merged_lo")
        s_xr = sem("s_x_reloaded")
        s_hrow = sem("s_h_rows")
        s_small3 = sem("s_router_loaded")
        s_sq3, s_var3, s_std3, s_xn2 = sem("s_h_squared"), sem("s_h_variance"), sem("s_h_std"), sem("s_xn2_ready")
        s_xn2g, s_xn2T, s_xn2c = sem("s_xn2_scaled"), sem("s_xn2_turned"), sem("s_xn2T_ready")
        s_logit, s_v5, s_store = sem("s_logits"), sem("s_vector_norm2"), sem("s_xn2_stored")

        p3_psum = ExitStack()
        PS3 = p3_psum.enter_context(nc.psum_tensor("PS3", [P, 2 * GT, GW], F32))
        nc.clear_and_free_semaphores(mixer_sems)

        with nc.Block() as block:
            @block.sync
            def _(sp):
                for g in range(N3):
                    for kq in range(2):
                        wait(sp, t_l, 2 * g + kq - 1)
                        sp.dma_start(raw3[:, kq, :, :], SOURCES[g][:, kq * GT:(kq + 1) * GT, :]).then_inc(t_raw[kq], 16)
                    if g == YA:
                        sp.wait_ge(s_ol, KD)
                        sp.dma_start(h_rows[:], x_d).then_inc(s_xr, 16)
                sp.wait_ge(t_l, 2 * N3)
                sp.dma_start(ffn_gain, norm_ffn_g[0].partition_broadcast(P)).then_inc(s_small3, 16)
                sp.dma_start(router_w, w_router[0].rearrange("(k p) e -> p k e", p=P)).then_inc(s_small3, 16)
                sp.dma_start(router_b, b_router[0].partition_broadcast(P)).then_inc(s_small3, 16)
                for t in range(TT):
                    sp.wait_ge(s_xn2, t + 1)
                    sp.dma_start(xn2_d.rearrange("(t p) d -> p t d", p=P)[:, t, :], xn2[:, t, :]).then_inc(s_store, 16)
                sp.wait_ge(s_store, 16 * TT)

            @block.scalar
            def _(act):
                def split(g):
                    for kq in range(2):
                        act.wait_ge(t_raw[kq], 16 * (g + 1))
                        wait(act, t_grp if kq else t_used, g)
                        nc.scalar.activation(hi3[:, kq, :, :], raw3[:, kq, :, :], ACT.Copy).then_inc(t_h, 1)

                split(0)
                for g in range(N3):
                    if g + 1 < N3:
                        split(g + 1)
                    if g == GATES + 1:
                        for k in range(KD):
                            nc.scalar.activation(out_hi[:, k, :], zT[:, k, :], ACT.Copy).then_inc(s_oh, 1)
                    act.wait_ge(t_grp, g + 1)
                    if g < YA:
                        gate = (gateA, gateB)[g % 2]
                        for j in range(GT):
                            nc.scalar.activation(gate[:, GT * (g // 2) + j, :], PS3[:, GT * (g % 2) + j, :],
                                                 ACT.Sigmoid).then_inc(t_bank[g % 2], 1)
                    if g == YA - 1:
                        for k in range(KD):
                            nc.scalar.activation(xT_hi[:, k, :], ybT[:, k, :], ACT.Copy).then_inc(s_yh, 1)
                    if YB <= g < MIX:
                        for j in range(GT):
                            k = GT * (g - YB) + j
                            act.wait_ge(s_merge, k + 1)
                            nc.scalar.activation(out_hi[:, k, :], gateA[:, k, :], ACT.Copy).then_inc(s_mh, 1)
                for t in range(TT):
                    act.wait_ge(s_hrow, TT + t + 1)
                    wait(act, s_sq3, t)
                    nc.scalar.activation(sq3, h_rows[:, t, :], ACT.Square, accum_out=stat3[:, 0, t:t + 1]).then_inc(s_sq3, 1)
                act.wait_ge(s_var3, 1)
                nc.scalar.activation(stat3[:, 2, :], stat3[:, 1, :], ACT.Sqrt).then_inc(s_std3, 1)
                for k in range(KD):
                    act.wait_ge(s_xn2T, k + 1)
                    nc.scalar.activation(xn2T[:, k, :], PS3[:, k, :], ACT.Copy).then_inc(s_xn2c, 1)

            @block.vector
            def _(dve):
                def split(g):
                    for kq in range(2):
                        dve.wait_ge(t_h, 2 * g + kq + 1)
                        nc.vector.tensor_tensor(lo3[:, kq, :, :], raw3[:, kq, :, :], hi3[:, kq, :, :].bitcast(F32),
                                                ALU.subtract).then_inc(t_l, 1)

                split(0)
                for g in range(N3):
                    if g + 1 < N3:
                        split(g + 1)
                    if g == GATES + 1:
                        for k in range(KD):
                            dve.wait_ge(s_oh, k + 1)
                            nc.vector.tensor_tensor(out_lo[:, k, :], zT[:, k, :], out_hi[:, k, :].bitcast(F32),
                                                    ALU.subtract).then_inc(s_ol, 1)
                    if g == YA - 1:
                        for k in range(KD):
                            dve.wait_ge(s_yh, k + 1)
                            nc.vector.tensor_tensor(xT_lo[:, k, :], ybT[:, k, :], xT_hi[:, k, :].bitcast(F32),
                                                    ALU.subtract).then_inc(s_yl, 1)
                    if g >= YA:
                        dve.wait_ge(t_grp, g + 1)
                    for j in range(GT):
                        k = GT * (g % 2) + j
                        bank = PS3[:, GT * (g % 2) + j, :]
                        if YA <= g < YB:
                            dve.wait_ge(t_bank[0], 2 * GT)
                            dve.wait_ge(t_bank[1], 2 * GT)
                            nc.vector.tensor_tensor(gateA[:, k, :], bank, gateA[:, k, :], ALU.mult).then_inc(t_bank[g % 2], 1)
                        elif YB <= g < MIX:
                            if k >= 2:
                                dve.wait_ge(s_merge, k - 1)
                            nc.vector.tensor_tensor(part[:, j % 2, :], bank, gateB[:, k, :], ALU.mult).then_inc(t_bank[g % 2], 1)
                            dve.wait_ge(t_bank[g % 2], GT * (g // 2) + j + 1)
                            nc.vector.tensor_tensor(gateA[:, k, :], gateA[:, k, :], part[:, j % 2, :],
                                                    ALU.add).then_inc(s_merge, 1)
                            dve.wait_ge(s_mh, k + 1)
                            nc.vector.tensor_tensor(out_lo[:, k, :], gateA[:, k, :], out_hi[:, k, :].bitcast(F32),
                                                    ALU.subtract).then_inc(s_ml, 1)
                        elif g >= MIX:
                            dve.wait_ge(s_xr, 16)
                            rows = h_rows[:, j, GW * (g - MIX):GW * (g - MIX + 1)]
                            nc.vector.tensor_tensor(rows, rows, bank, ALU.add).then_inc(s_hrow, 1)
                dve.wait_ge(s_sq3, TT)
                nc.vector.tensor_scalar(stat3[:, 1, :], stat3[:, 0, :], 1.0 / D, EPS, ALU.mult, ALU.add).then_inc(s_var3, 1)
                dve.wait_ge(s_std3, 1)
                nc.vector.reciprocal(stat3[:, 3, :], stat3[:, 2, :]).then_inc(s_v5, 1)
                dve.wait_ge(s_v5, 1)
                dve.wait_ge(s_small3, 48)
                for t in range(TT):
                    nc.vector.scalar_tensor_tensor(out=xn2[:, t, :], in0=h_rows[:, t, :], scalar=stat3[:, 3, t:t + 1],
                                                   in1=ffn_gain, op0=ALU.mult, op1=ALU.mult).then_inc(s_xn2, 1)
                dve.wait_ge(s_logit, 1)
                nc.vector.tensor_tensor(logits[:], PS3[:, 0, 0:TT * E].rearrange("p (t e) -> p t e", t=TT),
                                        router_b.unsqueeze(1).to_broadcast([P, TT, E]), ALU.add).then_inc(s_v5, 1)

            @block.tensor
            def _(pe):
                for g in range(N3):
                    if g < MIX:
                        wait(pe, t_bank[g % 2], GT * (g // 2))
                    else:
                        pe.wait_ge(t_bank[g % 2], GT * (MIX // 2))
                    if g == YA:
                        pe.wait_ge(s_ol, KD)
                    if g == YB:
                        pe.wait_ge(s_yl, KD)
                    r_hi, r_lo = (out_hi, out_lo) if YA <= g < YB else (xT_hi, xT_lo)
                    for kq in range(2):
                        pe.wait_ge(t_l, 2 * g + kq + 1)
                        for kk in range(GT):
                            k = GT * kq + kk
                            if g == MIX:
                                pe.wait_ge(s_ml, k + 1)
                            for j in range(GT):
                                dst = PS3[:, GT * (g % 2) + j, :]
                                if g < MIX:
                                    w_hi, w_lo = (w[:, kq, kk, j * P:(j + 1) * P] for w in (hi3, lo3))
                                    terms = ((w_hi, r_hi[:, k, :]), (w_hi, r_lo[:, k, :]), (w_lo, r_hi[:, k, :]))
                                else:
                                    m_hi, m_lo = (m[:, k, j * P:(j + 1) * P] for m in (out_hi, out_lo))
                                    terms = ((m_hi, hi3[:, kq, kk, :]), (m_hi, lo3[:, kq, kk, :]), (m_lo, hi3[:, kq, kk, :]))
                                for n, (lhsT, rhs) in enumerate(terms):
                                    mm = pe.matmul(dst, lhsT, rhs, start=(k == 0 and n == 0), stop=(k == KD - 1 and n == 2))
                                if k == KD - 1 and j == GT - 1:
                                    mm.then_inc(t_grp, 1)
                                elif kk == GT - 1 and j == GT - 1:
                                    mm.then_inc(t_used, 1)
                pe.wait_ge(s_xn2, TT)
                for k in range(KD):
                    for t in range(TT):
                        mm = pe.transpose(PS3[:, k, t * P:(t + 1) * P], xn2[:, t, k * P:(k + 1) * P], ident[:, :])
                    mm.then_inc(s_xn2T, 1)
                pe.wait_ge(s_xn2c, KD)
                for t in range(TT):
                    for k in range(KD):
                        mm = pe.matmul(PS3[:, 0, t * E:(t + 1) * E], xn2T[:, k, t * P:(t + 1) * P], router_w[:, k, :],
                                       start=(k == 0), stop=(k == KD - 1))
                mm.then_inc(s_logit, 1)
        p3_psum.close()
        p3.close()
        mixer.close()

        ITEMS = E * TT
        FF = w_down.shape[2]
        CH = 12
        RAW = 6
        SPL = 4
        K4 = TT * TOPK

        y_d = nc.dram_tensor("expert_rows_scratch", (SEQ * TOPK + P, D), F32, kind="Internal").ap()

        mraw = keep("mraw", [P, RAW, 2, 2, GW])
        bias = keep("bias", [2 * E, 3 * D], F32R)
        pick = keep("pick", [2 * E, E + 1])
        ones_row = keep("ones_row", [2 * E, P])
        index = keep("index", [P, ITEMS + 1], U32)
        target = keep("target", [P, ITEMS], U32)
        weight = keep("weight", [P, K4])
        more_items = keep("more_items", [P, 1], I32)

        route = ExitStack()

        def r_sb(name, shape, dt=F32):
            return route.enter_context(nc.sbuf_tensor(name, shape, dt))

        bias_raw = r_sb("bias_raw", [2 * E, 3 * D])
        iota_i = r_sb("iota_i", [P, P + TT + K4], I32)
        iota = r_sb("iota", [P, P + TT + K4])
        target_f = r_sb("target_f", [P, 2, ITEMS])
        ones = r_sb("ones", [P, P])
        top = r_sb("top", [P, TT, 8])
        top_i = r_sb("top_i", [P, TT, 8], U32)
        chosen = r_sb("chosen", [P, K4, E])
        taken = r_sb("taken", [P, TT, E])
        place = r_sb("place", [P, TT, E])
        at_place = r_sb("at_place", [P, K4, E])
        small = r_sb("small", [P, 12, K4])
        slot_is = r_sb("slot_is", [P, K4, P])
        item_is = r_sb("item_is", [P, K4, P])
        e_f, pos, blk, blk2, blk3, item, within, row, d4, ex4, tok4, sums = (small[:, n, :] for n in range(12))

        s_br, s_bh, s_bl = sem("s_bias_loaded"), sem("s_bias_hi"), sem("s_bias_lo")
        s_io, s_pk, s_on1 = sem("s_iotas"), sem("s_pick_ready"), sem("s_ones_ready")
        s_vr = sem("s_routing_step")
        s_taken, s_place, s_hot, s_idx = sem("s_taken_ready"), sem("s_places"), sem("s_one_hots"), sem("s_index_product")
        s_d4, s_ex4 = sem("s_top_diff"), sem("s_top_exp")
        s_mraw = [sem(f"s_weights_loaded{k}") for k in range(RAW)]

        PM = ctx.enter_context(nc.psum_tensor("PM", [P, 8, GW], F32))

        gu = w_gate_up[0].rearrange("e (q kk p) (two c) -> e q p kk two c", p=P, kk=2, two=2)
        dn = w_down[0].rearrange("e (q kk p) (two c) -> e q p kk two c", p=P, kk=2, two=2)

        def load_weights(sp, e, m):
            src, half = (gu, m // 4) if m < 8 else (dn, 0)
            for kk in range(2):
                one = src[bass.ds(e, 1), m % 4, :, kk].rearrange("a p two c -> (a p) two c")
                sp.dma_start(mraw[:, m % RAW, kk], one[:, :, half * GW:(half + 1) * GW]).then_inc(s_mraw[m % RAW], 16)

        with nc.Block() as block:
            @block.sync
            def _(sp):
                for half in range(2):
                    rows = slice(E * half, E * half + E)
                    sp.dma_start(bias_raw[rows, 0:2 * D], b_gate_up[0]).then_inc(s_br, 16)
                    sp.dma_start(bias_raw[rows, 2 * D:3 * D], b_down[0]).then_inc(s_br, 16)
                for m in range(RAW):
                    load_weights(sp, 0, m)

            @block.gpsimd
            def _(pool):
                nc.gpsimd.iota(iota_i[:, 0:P], [[1, P]], base=0, channel_multiplier=0).then_inc(s_io, 1)
                nc.gpsimd.iota(iota_i[:, P:P + TT], [[0, TT]], base=SEQ * TOPK, channel_multiplier=1).then_inc(s_io, 1)
                nc.gpsimd.iota(iota_i[:, P + TT:], [[TOPK * P, TT], [1, TOPK]], base=0, channel_multiplier=TOPK).then_inc(s_io, 1)
                nc.gpsimd.memset(ones[:], 1.0).then_inc(s_on1, 1)
                nc.gpsimd.memset(index[:], 0).then_inc(s_on1, 1)
                nc.gpsimd.memset(ones_row[:], 1.0).then_inc(s_on1, 1)
                pool.wait_ge(s_on1, 3)
                for n, (rows, first, dst) in enumerate(((slice(0, E), 0, 0), (slice(E, 2 * E), E, 0))):
                    nc.gpsimd.tensor_copy(pick[rows, 0:E], ident[rows, first:first + E]).then_inc(s_pk, 1)
                    pool.wait_ge(s_pk, 2 * n + 1)
                    nc.gpsimd.tensor_copy(pick[rows, E:E + 1], ident[rows, first:first + 1]).then_inc(s_pk, 1)
                    pool.wait_ge(s_pk, 2 * n + 2)

            @block.scalar
            def _(act):
                act.wait_ge(s_br, 64)
                nc.scalar.activation(bias[:], bias_raw[:], ACT.Copy).then_inc(s_bh, 1)
                act.wait_ge(s_d4, 1)
                nc.scalar.activation(ex4, d4, ACT.Exp).then_inc(s_ex4, 1)

            @block.vector
            def _(dve):
                steps = [0]

                def link(ins):
                    steps[0] += 1
                    ins.then_inc(s_vr, 1)
                    dve.wait_ge(s_vr, steps[0])

                def by_tile(tile):
                    return tile.rearrange("p (t k) -> p t k", t=TT)

                for t in range(TT):
                    link(nc.vector.max(top[:, t, :], logits[:, t, :]))
                    link(nc.vector.max_index(top_i[:, t, :], top[:, t, :], logits[:, t, :]))
                link(nc.vector.tensor_copy(by_tile(e_f), top_i[:, :, 0:TOPK]))
                dve.wait_ge(s_io, 3)
                link(nc.vector.tensor_copy(iota[:], iota_i[:]))
                link(nc.vector.tensor_tensor(chosen[:], iota[:, 0:E].unsqueeze(1).to_broadcast([P, K4, E]),
                                             e_f.unsqueeze(2).to_broadcast([P, K4, E]), ALU.is_equal))
                nc.vector.tensor_reduce(taken[:], chosen[:].rearrange("p (t k) e -> p t e k", t=TT), AX,
                                        ALU.add).then_inc(s_taken, 1)
                nc.vector.tensor_tensor(by_tile(d4), top[:, :, 0:TOPK], top[:, :, 0:1].to_broadcast([P, TT, TOPK]),
                                        ALU.subtract).then_inc(s_d4, 1)
                dve.wait_ge(s_ex4, 1)
                link(nc.vector.tensor_reduce(sums[:, 0:TT], by_tile(ex4), AX, ALU.add))
                link(nc.vector.reciprocal(sums[:, TT:2 * TT], sums[:, 0:TT]))
                link(nc.vector.tensor_tensor(by_tile(weight[:]), by_tile(ex4),
                                             sums[:, TT:2 * TT].unsqueeze(2).to_broadcast([P, TT, TOPK]), ALU.mult))
                dve.wait_ge(s_place, 1)
                link(nc.vector.tensor_copy(place[:], PM[:, 0, 0:TT * E].rearrange("p (t e) -> p t e", t=TT)))
                link(nc.vector.tensor_reduce(sums[:, 8:9], PM[:, 1, 0:E], AX, ALU.max))
                link(nc.vector.tensor_scalar(sums[:, 9:10], sums[:, 8:9], float(P), None, ALU.is_gt))
                for n in range(2, TT):
                    link(nc.vector.scalar_tensor_tensor(out=sums[:, 9:10], in0=sums[:, 8:9], scalar=float(n * P),
                                                        in1=sums[:, 9:10], op0=ALU.is_gt, op1=ALU.add))
                link(nc.vector.tensor_copy(more_items[:], sums[:, 9:10]))
                link(nc.vector.tensor_tensor(at_place[:].rearrange("p (t k) e -> p t k e", t=TT),
                                             chosen[:].rearrange("p (t k) e -> p t k e", t=TT),
                                             place[:].unsqueeze(2).to_broadcast([P, TT, TOPK, E]), ALU.mult))
                link(nc.vector.tensor_reduce(pos, at_place[:], AX, ALU.add))
                link(nc.vector.tensor_scalar(blk, pos, float(P), None, ALU.is_ge))
                link(nc.vector.scalar_tensor_tensor(out=blk2, in0=pos, scalar=2.0 * P, in1=blk, op0=ALU.is_ge, op1=ALU.add))
                link(nc.vector.scalar_tensor_tensor(out=blk3, in0=pos, scalar=3.0 * P, in1=blk2, op0=ALU.is_ge, op1=ALU.add))
                link(nc.vector.scalar_tensor_tensor(out=item, in0=blk3, scalar=float(E), in1=e_f, op0=ALU.mult, op1=ALU.add))
                link(nc.vector.scalar_tensor_tensor(out=within, in0=blk3, scalar=-float(P), in1=pos, op0=ALU.mult, op1=ALU.add))
                link(nc.vector.scalar_tensor_tensor(out=row, in0=within, scalar=-1.0, in1=iota[:, P + TT:P + TT + K4],
                                                    op0=ALU.mult, op1=ALU.add))
                link(nc.vector.tensor_scalar(tok4, row, -float(SEQ * TOPK), None, ALU.add))
                every = iota[:, 0:P].unsqueeze(1).to_broadcast([P, K4, P])
                link(nc.vector.tensor_tensor(slot_is[:], every, within.unsqueeze(2).to_broadcast([P, K4, P]), ALU.is_equal))
                link(nc.vector.tensor_tensor(item_is[:], every, item.unsqueeze(2).to_broadcast([P, K4, P]), ALU.is_equal))
                nc.vector.tensor_tensor(item_is[:], item_is[:], tok4.unsqueeze(2).to_broadcast([P, K4, P]),
                                        ALU.mult).then_inc(s_hot, 1)
                dve.wait_ge(s_bh, 1)
                nc.vector.tensor_tensor(bias[E:2 * E, :], bias_raw[E:2 * E, :], bias[E:2 * E, :].bitcast(F32),
                                        ALU.subtract).then_inc(s_bl, 1)
                dve.wait_ge(s_idx, 1)
                dve.wait_ge(s_on1, 3)
                link(nc.vector.tensor_scalar(target_f[:, 0, :], PM[:, 2, 0:ITEMS], iota[:, P:P + 1], None, ALU.add))
                link(nc.vector.tensor_copy(target[:], target_f[:, 0, :]))
                link(nc.vector.tensor_scalar(target_f[:, 1, :], target_f[:, 0, :], float(SEQ * TOPK - 1), None, ALU.min))
                link(nc.vector.tensor_copy(index[:, 0:ITEMS], target_f[:, 1, :]))
                link(nc.vector.tensor_scalar(index[:, 0:ITEMS], index[:, 0:ITEMS], 2, None, ALU.logical_shift_right))

            @block.tensor
            def _(pe):
                pe.wait_ge(s_taken, 1)
                pe.wait_ge(s_on1, 3)
                for t in range(TT):
                    for before in range(t + 1):
                        pe.matmul(PM[:, 0, t * E:(t + 1) * E], strict[:, :] if before == t else ones[:, :],
                                  taken[:, before, :], start=(before == 0), stop=(before == t))
                for t in range(TT):
                    mm = pe.matmul(PM[:, 1, 0:E], ones[:, :], taken[:, t, :], start=(t == 0), stop=(t == TT - 1))
                mm.then_inc(s_place, 1)
                pe.wait_ge(s_hot, 1)
                for n in range(K4):
                    mm = pe.matmul(PM[:, 2, 0:ITEMS], slot_is[:, n, :], item_is[:, n, :], start=(n == 0), stop=(n == K4 - 1))
                mm.then_inc(s_idx, 1)
        route.close()

        mhi = keep("mhi", [P, SPL, 2, 2, GW], F32R)
        mlo = keep("mlo", [P, SPL, 2, 2, GW], F32R)
        expert = keep("expert", [2 * E, P], F32R)
        now = keep("now", [P, 2], U32)
        xg = keep("xg", [P, D])
        xgT_hi = keep("xgT_hi", [P, KD, P], F32R)
        xgT_lo = keep("xgT_lo", [P, KD, P], F32R)
        glu = keep("glu", [P, 2, 4, GW])
        hT_hi = keep("hT_hi", [P, KD, P], F32R)
        hT_lo = keep("hT_lo", [P, KD, P], F32R)
        y_rows = keep("y_rows", [P, D])
        idle = keep("idle", [P, 2])
        LIMIT, ALPHA = 7.0, 1.702
        HALF = KD // 2

        e_h, e_l, e_used = sem("s_weights_hi"), sem("s_weights_lo"), sem("s_weights_used")
        s_now, s_xg, s_tx = sem("s_index_copied"), sem("s_tokens_gathered"), sem("s_tokens_turned")
        s_gh, s_gl = sem("s_tokens_hi"), sem("s_tokens_lo")
        s_exp2 = sem("s_expert_picked")
        s_gate, s_up, s_sig, s_prod, s_hid = (sem("s_gate_clamped"), sem("s_up_clamped"), sem("s_gate_sigmoid"),
                                              sem("s_gate_times_up"), sem("s_hidden"))
        s_th, s_hh, s_hl = sem("s_hidden_turned"), sem("s_hidden_hi"), sem("s_hidden_lo")
        s_y, s_yst, s_goal = sem("s_y_rows"), sem("s_y_stored"), sem("s_target_copied")
        s_yfree, s_idle = sem("s_y_rows_free"), sem("s_idle_step")

        def last_item(eng):
            return eng.value_load(more_items[0:1, 0:1], min_val=0, max_val=TT - 1) * E + (E - 1)

        def all_items(eng, body):
            more = eng.value_load(more_items[0:1, 0:1], min_val=0, max_val=TT - 1)
            with eng.Fori(0, more + 1) as b:
                with eng.Fori(0, E) as e:
                    body(b * E + e, e)

        with nc.Block() as block:
            @block.sync
            def _(sp):
                last = last_item(sp)

                def load(i, m):
                    sp.wait_ge(e_l, CH * i + m - RAW + 1)
                    load_weights(sp, i % E, m)

                with sp.Fori(0, last) as i:
                    for m in range(RAW, CH):
                        load(i, m)
                    for m in range(RAW):
                        load(i + 1, m)
                for m in range(RAW, CH):
                    sp.wait_ge(e_l, CH * last + m - RAW + 1)
                    load_weights(sp, E - 1, m)
                for m in range(3):
                    sp.wait_ge(e_l, CH * last + CH - RAW + m + 1)
                    sp.sem_inc(s_mraw[m], 32)

            @block.gpsimd
            def _(pool):
                def step():
                    nc.gpsimd.tensor_tensor(idle[:, 0:1], idle[:, 1:2], idle[:, 1:2], ALU.add).then_inc(s_idle, 1)

                nc.gpsimd.memset(idle[:], 0.0).then_inc(s_idle, 1)
                pool.wait_ge(s_idle, 1)
                pool.sem_inc(s_yfree, 1)

                def gather(i):
                    nc.gpsimd.tensor_copy(now[:, 0:1], index[:, bass.ds(i, 1)]).then_inc(s_now, 1)
                    pool.wait_ge(s_now, i + 1)
                    step()
                    nc.gpsimd.indirect_dma_start(xg[:], None, xn2_d, bass.IndirectOffsetOnAxis(ap=now[:, 0:1], axis=0)
                                                 ).then_inc(s_xg, 16)

                gather(0)

                def body(i, e):
                    pool.wait_ge(s_tx, i + 1)
                    gather(i + 1)
                    for half in range(2):
                        pool.wait_ge(s_prod, 2 * i + half + 1)
                        pool.wait_ge(s_sig, 2 * i + half + 1)
                        nc.gpsimd.tensor_tensor(glu[:, half, 3, :], glu[:, half, 1, :], glu[:, half, 2, :],
                                                ALU.mult).then_inc(s_hid, 1)
                    nc.gpsimd.tensor_copy(now[:, 1:2], target[:, bass.ds(i, 1)]).then_inc(s_goal, 1)
                    pool.wait_ge(s_goal, i + 1)
                    pool.wait_ge(s_y, 2 * i + 3)
                    step()
                    nc.gpsimd.indirect_dma_start(y_d, bass.IndirectOffsetOnAxis(ap=now[:, 1:2], axis=0), y_rows[:], None
                                                 ).then_inc(s_yst, 16)
                    pool.wait_ge(s_yst, 16 * i + 16)
                    pool.sem_inc(s_yfree, 1)

                all_items(pool, body)

            @block.scalar
            def _(act):
                act.sem_inc(e_used, SPL)
                act.sem_inc(s_y, 1)

                def split(i, m):
                    act.wait_ge(s_mraw[m % RAW], 64 * i + 32 * (m // RAW) + 32)
                    act.wait_ge(e_used, CH * i + m + 1)
                    nc.scalar.activation(mhi[:, m % SPL], mraw[:, m % RAW], ACT.Copy).then_inc(e_h, 1)

                def tokens_hi(i):
                    for q in range(2):
                        act.wait_ge(s_tx, i + 1)
                        nc.scalar.activation(xgT_hi[:, HALF * q:HALF * (q + 1), :], PM[:, q, :].rearrange("p (k s) -> p k s", s=P),
                                             ACT.Copy).then_inc(s_gh, 1)

                def sigmoid(i, half):
                    act.wait_ge(s_gate, 2 * i + half + 1)
                    nc.scalar.activation(glu[:, half, 2, :], glu[:, half, 0, :], ACT.Sigmoid, scale=ALPHA).then_inc(s_sig, 1)

                def hidden_hi(i, half):
                    act.wait_ge(s_th, 2 * i + half + 1)
                    nc.scalar.activation(hT_hi[:, HALF * half:HALF * (half + 1), :],
                                         PM[:, 6 + half, :].rearrange("p (k s) -> p k s", s=P), ACT.Copy).then_inc(s_hh, 1)

                nc.scalar.activation(expert[:], ones_row[:], ACT.Copy, scale=pick[:, 0:1]).then_inc(s_exp2, 1)
                for m in range(3):
                    split(0, m)
                tokens_hi(0)

                def body(i, e):
                    for m in range(3, 8):
                        split(i, m)
                    sigmoid(i, 0)
                    split(i, 8)
                    split(i, 9)
                    split(i, 10)
                    hidden_hi(i, 0)
                    split(i, 11)
                    sigmoid(i, 1)
                    split(i + 1, 0)
                    hidden_hi(i, 1)
                    tokens_hi(i + 1)
                    split(i + 1, 1)
                    split(i + 1, 2)
                    act.wait_ge(e_used, CH * (i + 1) + SPL)
                    nc.scalar.activation(expert[:], ones_row[:], ACT.Copy, scale=pick[:, bass.ds(e + 1, 1)]).then_inc(s_exp2, 1)
                    act.wait_ge(s_yfree, i + 1)
                    for half in range(2):
                        nc.scalar.activation(y_rows[:, GW * half:GW * (half + 1)], PM[:, 4 + half, :], ACT.Copy).then_inc(s_y, 1)

                all_items(act, body)

            @block.vector
            def _(dve):
                def split(i, m):
                    dve.wait_ge(e_h, CH * i + m + 1)
                    nc.vector.tensor_tensor(mlo[:, m % SPL], mraw[:, m % RAW], mhi[:, m % SPL].bitcast(F32),
                                            ALU.subtract).then_inc(e_l, 1)

                def tokens_lo(i):
                    for q in range(2):
                        dve.wait_ge(s_gh, 2 * i + q + 1)
                        part_of = slice(HALF * q, HALF * (q + 1))
                        nc.vector.tensor_tensor(xgT_lo[:, part_of, :], PM[:, q, :].rearrange("p (k s) -> p k s", s=P),
                                                xgT_hi[:, part_of, :].bitcast(F32), ALU.subtract).then_inc(s_gl, 1)

                def clamp(i, half):
                    dve.wait_ge(e_used, CH * i + 4 * (half + 1) + SPL)
                    nc.vector.tensor_scalar(glu[:, half, 0, :], PM[:, 2 * half, :], LIMIT, None, ALU.min).then_inc(s_gate, 1)
                    nc.vector.tensor_scalar(glu[:, half, 1, :], PM[:, 2 * half + 1, :], LIMIT, -LIMIT, ALU.min,
                                            ALU.max).then_inc(s_up, 1)

                def gated(i, half):
                    dve.wait_ge(s_up, 2 * i + half + 1)
                    nc.vector.scalar_tensor_tensor(out=glu[:, half, 1, :], in0=glu[:, half, 1, :], scalar=1.0,
                                                   in1=glu[:, half, 0, :], op0=ALU.add, op1=ALU.mult).then_inc(s_prod, 1)

                def hidden_lo(i, half):
                    dve.wait_ge(s_hh, 2 * i + half + 1)
                    part_of = slice(HALF * half, HALF * (half + 1))
                    nc.vector.tensor_tensor(hT_lo[:, part_of, :], PM[:, 6 + half, :].rearrange("p (k s) -> p k s", s=P),
                                            hT_hi[:, part_of, :].bitcast(F32), ALU.subtract).then_inc(s_hl, 1)

                for m in range(3):
                    split(0, m)
                tokens_lo(0)

                def body(i, e):
                    for m in range(3, 8):
                        split(i, m)
                    clamp(i, 0)
                    gated(i, 0)
                    split(i, 8)
                    split(i, 9)
                    split(i, 10)
                    hidden_lo(i, 0)
                    clamp(i, 1)
                    gated(i, 1)
                    split(i, 11)
                    split(i + 1, 0)
                    hidden_lo(i, 1)
                    tokens_lo(i + 1)
                    split(i + 1, 1)
                    split(i + 1, 2)

                all_items(dve, body)

            @block.tensor
            def _(pe):
                def turn_tokens(i):
                    pe.wait_ge(s_xg, 16 * i + 16)
                    for k in range(KD):
                        mm = pe.transpose(PM[:, k // HALF, (k % HALF) * P:(k % HALF + 1) * P], xg[:, k * P:(k + 1) * P], ident[:, :])
                    mm.then_inc(s_tx, 1)

                def turn_hidden(i, half):
                    pe.wait_ge(s_hid, 2 * i + half + 1)
                    for k in range(HALF):
                        mm = pe.transpose(PM[:, 6 + half, k * P:(k + 1) * P], glu[:, half, 3, k * P:(k + 1) * P], ident[:, :])
                    mm.then_inc(s_th, 1)

                def start_with_bias(bank, first):
                    for n in range(2):
                        pe.matmul(PM[:, bank + n, :], expert[:, :], bias[:, first[n]:first[n] + GW], start=True, stop=False)

                def chunk(i, m, bank, t_hi, t_lo):
                    pe.wait_ge(e_l, CH * i + m + 1)
                    w_hi, w_lo = mhi[:, m % SPL], mlo[:, m % SPL]
                    for kk in range(2):
                        k = 2 * (m % 4) + kk
                        for n in range(2):
                            pe.matmul(PM[:, bank + n, :], t_hi[:, k, :], w_hi[:, kk, n, :], start=False, stop=False)
                            pe.matmul(PM[:, bank + n, :], t_hi[:, k, :], w_lo[:, kk, n, :], start=False, stop=False)
                        for n in range(2):
                            mm = pe.matmul(PM[:, bank + n, :], t_lo[:, k, :], w_hi[:, kk, n, :], start=False, stop=(k == KD - 1))
                    mm.then_inc(e_used, 1)

                turn_tokens(0)

                def body(i, e):
                    pe.wait_ge(s_gl, 2 * i + 2)
                    pe.wait_ge(s_exp2, i + 1)
                    start_with_bias(0, (0, D))
                    for m in range(4):
                        chunk(i, m, 0, xgT_hi, xgT_lo)
                    start_with_bias(2, (GW, D + GW))
                    for m in range(4, 7):
                        chunk(i, m, 2, xgT_hi, xgT_lo)
                    turn_hidden(i, 0)
                    chunk(i, 7, 2, xgT_hi, xgT_lo)
                    pe.wait_ge(s_y, 2 * i + 1)
                    start_with_bias(4, (2 * D, 2 * D + GW))
                    pe.wait_ge(s_hl, 2 * i + 1)
                    chunk(i, 8, 4, hT_hi, hT_lo)
                    chunk(i, 9, 4, hT_hi, hT_lo)
                    turn_hidden(i, 1)
                    turn_tokens(i + 1)
                    pe.wait_ge(s_hl, 2 * i + 2)
                    chunk(i, 10, 4, hT_hi, hT_lo)
                    chunk(i, 11, 4, hT_hi, hT_lo)

                all_items(pe, body)

        rows_t = [mraw[:, 2 * n:2 * n + 2].rearrange("p s a b c -> p (s a b c)").rearrange("p (k d) -> p k d", k=TOPK)
                  for n in range(2)]
        final_gain = mraw[:, 4, 0].rearrange("p b c -> p (b c)")
        y_by_token = y_d[0:SEQ * TOPK, :].rearrange("(t p k) d -> t p (k d)", p=P, k=TOPK)
        s_fg, s_pick = sem("s_final_gain"), [sem(f"s_rows_back{k}") for k in range(2)]
        s_added, s_fsq, s_fvar, s_fstd, s_frec, s_out, s_st = (
            sem("s_row_added"), sem("s_final_squares"), sem("s_final_variance"), sem("s_final_std"),
            sem("s_final_rstd"), sem("s_out_ready"), sem("s_out_stored"))
        fstat = glu[:, 0, 0, 0:16].rearrange("p (n t) -> p n t", n=4)
        fsq = glu[:, 1, 0:2, :].rearrange("p a c -> p (a c)")

        with nc.Block() as block:
            @block.sync
            def _(sp):
                sp.dma_start(final_gain, norm_final_g.partition_broadcast(P)).then_inc(s_fg, 16)
                sp.wait_ge(s_yst, last_item(sp) * 16 + 16)
                for t in range(TT):
                    wait(sp, s_added, TOPK * (t - 1))
                    for half in range(2):
                        w = slice(half * 2 * D, (half + 1) * 2 * D)
                        sp.dma_start(rows_t[t % 2].rearrange("p k d -> p (k d)")[:, w], y_by_token[t][:, w]
                                     ).then_inc(s_pick[t % 2], 16)
                for t in range(TT):
                    sp.wait_ge(s_out, t + 1)
                    sp.dma_start(out_d[:, t, :], h_rows[:, t, :]).then_inc(s_st, 16)
                sp.wait_ge(s_st, 16 * TT)

            @block.scalar
            def _(act):
                for t in range(TT):
                    act.wait_ge(s_added, TOPK * (t + 1))
                    wait(act, s_fsq, t)
                    nc.scalar.activation(fsq, h_rows[:, t, :], ACT.Square, accum_out=fstat[:, 0, t:t + 1]).then_inc(s_fsq, 1)
                    act.wait_ge(s_fvar, t + 1)
                    nc.scalar.activation(fstat[:, 2, t:t + 1], fstat[:, 1, t:t + 1], ACT.Sqrt).then_inc(s_fstd, 1)

            @block.vector
            def _(dve):
                def finish(t):
                    dve.wait_ge(s_fsq, t + 1)
                    nc.vector.tensor_scalar(fstat[:, 1, t:t + 1], fstat[:, 0, t:t + 1], 1.0 / D, EPS, ALU.mult,
                                            ALU.add).then_inc(s_fvar, 1)
                    dve.wait_ge(s_fstd, t + 1)
                    nc.vector.reciprocal(fstat[:, 3, t:t + 1], fstat[:, 2, t:t + 1]).then_inc(s_frec, 1)
                    dve.wait_ge(s_frec, t + 1)
                    dve.wait_ge(s_fg, 16)
                    nc.vector.scalar_tensor_tensor(out=h_rows[:, t, :], in0=h_rows[:, t, :], scalar=fstat[:, 3, t:t + 1],
                                                   in1=final_gain, op0=ALU.mult, op1=ALU.mult).then_inc(s_out, 1)

                for t in range(TT):
                    for k in range(TOPK):
                        n = t * TOPK + k
                        dve.wait_ge(s_pick[t % 2], 32 * (t // 2 + 1))
                        wait(dve, s_added, n)
                        nc.vector.scalar_tensor_tensor(out=h_rows[:, t, :], in0=rows_t[t % 2][:, k, :],
                                                       scalar=weight[:, n:n + 1], in1=h_rows[:, t, :], op0=ALU.mult,
                                                       op1=ALU.add).then_inc(s_added, 1)
                    if t >= 1:
                        finish(t - 1)
                finish(TT - 1)


_INS = ["x", "norm_mix_g", "w_in", "gdn_conv_w", "gdn_A_log", "gdn_dt_bias", "gdn_norm_g", "w_o_gdn", "sconv_w",
        "w_o_sconv", "w_mix_out", "norm_ffn_g", "w_router", "b_router", "w_gate_up", "b_gate_up", "w_down",
        "b_down", "norm_final_g"]


def kernel(**inputs):
    import numpy as _np
    import concourse.bacc as _bacc
    from concourse.bass_utils import run_bass_kernel_spmd as _run

    nc = _bacc.Bacc("TRN2", target_bir_lowering=False, num_devices=1)
    arrays, args = {}, []
    for name in _INS:
        a = _np.ascontiguousarray(inputs[name])
        arrays[f"in_{name}_dram"] = a
        args.append(nc.dram_tensor(f"in_{name}_dram", a.shape, mybir.dt.from_np(a.dtype), kind="ExternalInput").ap())
    out = nc.dram_tensor("out_0_dram", inputs["x"].shape, F32, kind="ExternalOutput").ap()
    hybrid_block(nc, *args, out)
    r = _run(nc, [arrays], core_ids=[0])
    return r.results[0]["out_0_dram"]
```

```python
from contextlib import ExitStack

import concourse.bass as bass
from concourse import mybir

ALU = mybir.AluOpType
ACT = mybir.ActivationFunctionType
AX = mybir.AxisListType.X
F32 = mybir.dt.float32
F32R = mybir.dt.float32r
I32 = mybir.dt.int32
U32 = mybir.dt.uint32

P = 128


def wait(eng, sem, value):
    if not isinstance(value, int) or value > 0:
        eng.wait_ge(sem, value)


def col(ap):
    return ap.rearrange("(n a) -> n a", a=1)


def hybrid_block(nc, x, norm_mix_g, w_in, gdn_conv_w, gdn_A_log, gdn_dt_bias, gdn_norm_g, w_o_gdn,
                 sconv_w, w_o_sconv, w_mix_out, norm_ffn_g, w_router, b_router, w_gate_up,
                 b_gate_up, w_down, b_down, norm_final_g, out):
    _, SEQ, D = x.shape
    TT = SEQ // P
    KD = D // P
    HEADS = gdn_A_log.shape[1]
    QKV = gdn_conv_w.shape[2] // P
    CONV = gdn_conv_w.shape[1]
    SCONV = sconv_w.shape[1]
    E = w_router.shape[2]
    TOPK = 4
    EPS = 1e-6
    GW = 512
    GT = GW // P
    assert QKV == 3 * HEADS and D == 2 * GW and KD == 8

    x_d = x[0].rearrange("(t p) d -> p t d", p=P)
    out_d = out[0].rearrange("(t p) d -> p t d", p=P)
    w_in_d = w_in[0]
    Z0 = QKV * P
    A0 = Z0 + D
    B0 = A0 + HEADS
    XS0 = B0 + HEADS
    GB0, GC0, GA0, GBB0 = XS0 + D, XS0 + 2 * D, XS0 + 3 * D, XS0 + 4 * D

    xn2_d = nc.dram_tensor("xn2_scratch", (SEQ, D), F32, kind="Internal").ap()

    with ExitStack() as ctx:
        def sem(name):
            return ctx.enter_context(nc.semaphore(name))

        mixer_sems = []

        def mixer_sem(name):
            mixer_sems.append(nc.alloc_semaphore(name=name))
            return mixer_sems[-1]

        def keep(name, shape, dt=F32):
            return ctx.enter_context(nc.sbuf_tensor(name, shape, dt))

        ident = keep("ident", [P, P])
        tri = keep("tri", [P, P])
        strict = keep("strict", [P, P])
        LEVELS = 7
        pair_mask = keep("pair_mask", [P, LEVELS, P])
        cols = keep("cols", [P, P])
        gdn_gain = keep("gdn_gain", [P, 1])
        ab = keep("ab", [P, SEQ])
        decay_rate = keep("decay_rate", [P, 1])
        dt_bias = keep("dt_bias", [P, 1])
        zT = keep("zT", [P, HEADS, SEQ])
        logits = keep("logits", [P, TT, E])
        top = keep("top", [P, TT, 8])
        top_i = keep("top_i", [P, TT, 8], U32)

        def tap_of(j, tile):
            return cols[:, bass.ds(tile + j * QKV, 1)]

        def sconv_tap(j, c):
            n = CONV * QKV + j * KD + c
            return cols[:, n:n + 1]

        def mix_gain(k):
            n = CONV * QKV + SCONV * KD + k
            return cols[:, n:n + 1]

        mixer = ctx.enter_context(ExitStack())

        def mix_sb(name, shape, dt=F32):
            return mixer.enter_context(nc.sbuf_tensor(name, shape, dt))

        xT_hi = mix_sb("xT_hi", [P, KD, SEQ], F32R)
        xT_lo = mix_sb("xT_lo", [P, KD, SEQ], F32R)
        ybT = mix_sb("ybT", [P, KD, SEQ])

        front = ctx.enter_context(ExitStack())

        def front_sb(name, shape, dt=F32):
            return front.enter_context(nc.sbuf_tensor(name, shape, dt))

        qkvT = front_sb("qkvT", [P, QKV, SEQ])
        p1 = ExitStack()

        def p1_sb(name, shape, dt=F32):
            return p1.enter_context(nc.sbuf_tensor(name, shape, dt))

        raw = p1_sb("raw", [P, 2, GT, GW])
        hi = p1_sb("hi", [P, 2, GT, GW], F32R)
        lo = p1_sb("lo", [P, 2, GT, GW], F32R)
        wab_hi = p1_sb("wab_hi", [P, KD, P], F32R)
        wab_lo = p1_sb("wab_lo", [P, KD, P], F32R)
        gbT = p1_sb("gbT", [P, GT, SEQ])
        acc = p1_sb("acc", [P, 2, SEQ])
        mprod = p1_sb("mprod", [P, 1, SEQ])
        stat = p1_sb("stat", [P, 3, TT])
        x_rows = qkvT[:, 0:8, :].rearrange("p a b -> p (a b)").rearrange("p (t d) -> p t d", t=TT)
        squares = qkvT[:, 8:16, :].rearrange("p a b -> p (a b)").rearrange("p (t d) -> p t d", t=TT)
        small_rows = qkvT[:, 16, 0:P]
        wab_raw = qkvT[:, 18:20, :].rearrange("p a b -> p (a b)").rearrange("p (k c) -> p k c", k=KD)
        sp_s, sp_e, sp_n = (t[0:HEADS] for t in (mprod[:, 0, :], qkvT[:, 22, :], qkvT[:, 23, :]))
        level_mask = qkvT[:, 20:22, :].rearrange("p a b -> p (a b)").rearrange("p (l c) -> p l c", l=8)

        FIRST_COL = [XS0, GB0, GC0, XS0 + GW, GB0 + GW, GC0 + GW, Z0, Z0 + GW]
        FLAT = len(FIRST_COL)
        QKV_GROUPS = QKV // GT

        s_rows = mixer_sem("s_rows_loaded")
        s_const = mixer_sem("s_constants_loaded")
        s_ab_raw = mixer_sem("s_ab_weights_loaded")
        s_x = [mixer_sem(f"s_x_loaded{t}") for t in range(TT)]
        s_raw = [mixer_sem(f"s_raw_loaded{k}") for k in range(2)]
        s_h = mixer_sem("s_hi_ready")
        s_l = mixer_sem("s_lo_ready")
        s_used = mixer_sem("s_chunk_used")
        s_grp = mixer_sem("s_group_done")
        s_tap = mixer_sem("s_last_tap_done")
        s_tile = mixer_sem("s_last_group_tile_done")
        s_bank = [mixer_sem(f"s_banks_read{k}") for k in range(2)]
        s_k = mixer_sem("s_masks")
        s_ab_zero = mixer_sem("s_ab_weights_zeroed")
        s_sq = mixer_sem("s_squares_summed")
        s_var = mixer_sem("s_variance_ready")
        s_std = mixer_sem("s_std_ready")
        s_xs = mixer_sem("s_x_scaled")
        s_colT = mixer_sem("s_cols_turned")
        s_col = mixer_sem("s_cols_ready")
        s_xT = mixer_sem("s_x_turned")
        s_xh = mixer_sem("s_xT_hi_ready")
        s_xl = mixer_sem("s_xT_lo_ready")
        s_yb = mixer_sem("s_yb_ready")
        s_silu = mixer_sem("s_silu_done")
        s_z = mixer_sem("s_z_ready")
        s_abh = mixer_sem("s_ab_hi_ready")
        s_abl = mixer_sem("s_ab_lo_ready")
        s_abp = mixer_sem("s_ab_projected")
        s_ab = mixer_sem("s_ab_ready")
        s_abr, s_dact, s_dvec = mixer_sem("s_ab_gates_ready"), mixer_sem("s_decay_act"), mixer_sem("s_decay_vector")
        s_v = mixer_sem("s_vector_step")

        p1_psum = ExitStack()
        PS = p1_psum.enter_context(nc.psum_tensor("PS", [P, 2 * GT, GW], F32))
        w_in_k = w_in_d.rearrange("(k p) c -> p k c", p=P)

        with nc.Block() as block:
            @block.sync
            def _(sp):
                n = 0
                for src, rows in ((gdn_conv_w[0].rearrange("j (c p) -> (j c) p", p=P), CONV * QKV),
                                  (sconv_w[0].rearrange("j (c p) -> (j c) p", p=P), SCONV * KD),
                                  (norm_mix_g[0].rearrange("(c p) -> c p", p=P), KD)):
                    sp.dma_start(small_rows[n:n + rows, :], src).then_inc(s_rows, 16)
                    n += rows
                for t in range(TT):
                    sp.dma_start(x_rows[:, t, :], x_d[:, t, :]).then_inc(s_x[t], 16)

                def load(g, column):
                    for kq in range(2):
                        wait(sp, s_l, 2 * g + kq - 1)
                        src = w_in_k[:, kq * GT:(kq + 1) * GT, bass.ds(column, GW)]
                        sp.dma_start(raw[:, kq, :, :], src).then_inc(s_raw[kq], 16)

                load(0, FIRST_COL[0])
                sp.wait_ge(s_ab_zero, 1)
                for first, part in ((A0, 0), (B0, 32)):
                    sp.dma_start(wab_raw[:, :, part:part + HEADS],
                                 w_in_k[:, :, first:first + HEADS]).then_inc(s_ab_raw, 16)
                sp.dma_start(gdn_gain[:, :], col(gdn_norm_g[0])).then_inc(s_const, 16)
                sp.dma_start(decay_rate[0:HEADS, :], col(gdn_A_log[0])).then_inc(s_const, 16)
                sp.dma_start(dt_bias[0:HEADS, :], col(gdn_dt_bias[0])).then_inc(s_const, 16)
                for g in range(1, FLAT):
                    load(g, FIRST_COL[g])
                with sp.Fori(0, QKV_GROUPS) as q:
                    load(q + FLAT, q * GW)

            @block.gpsimd
            def _(pool):
                for tile, value in ((ident, 0.0), (tri, 1.0), (strict, 1.0), (level_mask, 1.0)):
                    nc.gpsimd.memset(tile[:], value).then_inc(s_k, 1)
                nc.gpsimd.memset(wab_raw[:], 0.0).then_inc(s_ab_zero, 1)
                pool.wait_ge(s_k, 4)
                nc.gpsimd.affine_select(out=ident[:], in_=ident[:], compare_op=ALU.not_equal, fill=1.0, base=0,
                                        pattern=[[-1, P]], channel_multiplier=1).then_inc(s_k, 1)
                nc.gpsimd.affine_select(out=tri[:], in_=tri[:], compare_op=ALU.is_ge, fill=0.0, base=0,
                                        pattern=[[1, P]], channel_multiplier=-1).then_inc(s_k, 1)
                nc.gpsimd.affine_select(out=strict[:], in_=strict[:], compare_op=ALU.is_gt, fill=0.0, base=0,
                                        pattern=[[1, P]], channel_multiplier=-1).then_inc(s_k, 1)
                for lv in range(LEVELS):
                    n = 1 << lv
                    block_of = level_mask[:, lv, :].rearrange("p (b r) -> p b r", r=n)
                    nc.gpsimd.affine_select(out=block_of, in_=block_of, compare_op=ALU.is_ge, fill=0.0, base=0,
                                            pattern=[[-n, P // n], [0, n]], channel_multiplier=1).then_inc(s_k, 1)
                    pool.wait_ge(s_k, 8 + 2 * lv)
                    nc.gpsimd.affine_select(out=block_of, in_=block_of, compare_op=ALU.is_ge, fill=0.0, base=n - 1,
                                            pattern=[[n, P // n], [0, n]], channel_multiplier=-1).then_inc(s_k, 1)
                pool.wait_ge(s_k, 7 + 2 * LEVELS)
                nc.gpsimd.tensor_tensor(pair_mask[:], level_mask[:, 1:8, :], level_mask[:, 0:7, :],
                                        ALU.subtract).then_inc(s_k, 1)

            @block.scalar
            def _(act):
                def std(t):
                    act.wait_ge(s_var, t + 1)
                    nc.scalar.activation(stat[:, 2, t:t + 1], stat[:, 1, t:t + 1], ACT.Sqrt).then_inc(s_std, 1)

                for t in range(TT):
                    act.wait_ge(s_x[t], 16)
                    nc.scalar.activation(squares[:, t, :], x_rows[:, t, :], ACT.Square,
                                         accum_out=stat[:, 0, t:t + 1]).then_inc(s_sq, 1)
                    if t >= 1:
                        std(t - 1)
                std(TT - 1)
                act.wait_ge(s_col, 1)

                def turned(tiles):
                    for k in tiles:
                        act.wait_ge(s_xT, k + 1)
                        nc.scalar.activation(xT_hi[:, k, :], PS[:, k, :], ACT.Copy, scale=mix_gain(k)).then_inc(s_xh, 1)

                def split(g, parts=range(2)):
                    for kq in parts:
                        act.wait_ge(s_raw[kq], 16 * (g + 1))
                        wait(act, s_grp if kq else s_used, g)
                        nc.scalar.activation(hi[:, kq, :, :], raw[:, kq, :, :], ACT.Copy).then_inc(s_h, 1)

                split(0, [0])
                turned(range(KD))
                split(0, [1])
                act.wait_ge(s_ab_raw, 32)
                nc.scalar.activation(wab_hi[:], wab_raw[:], ACT.Copy).then_inc(s_abh, 1)
                for g in range(FLAT):
                    split(g + 1)
                    if g in (2, 5):
                        continue
                    act.wait_ge(s_grp, g + 1)
                    if g == 4:
                        act.wait_ge(s_yb, GT)
                    for j in range(GT):
                        if g in (0, 3):
                            dst, func = ybT[:, GT * (g // 3) + j, :], ACT.Copy
                        elif g in (1, 4):
                            dst, func = gbT[:, j, :], ACT.Copy
                        else:
                            dst, func = zT[:, GT * (g - 6) + j, :], ACT.Silu
                        nc.scalar.activation(dst, PS[:, GT * (g % 2) + j, :], func).then_inc(s_bank[g % 2], 1)
                act.wait_ge(s_abp, 1)
                nc.scalar.activation(ab[:, :], PS[:, 0, :], ACT.Copy).then_inc(s_ab, 1)
                act.wait_ge(s_ab, 1)
                nc.scalar.activation(ab[32:32 + HEADS, :], ab[32:32 + HEADS, :], ACT.Sigmoid).then_inc(s_abr, 1)
                act.wait_ge(s_const, 48)
                nc.scalar.activation(decay_rate[0:HEADS, :], decay_rate[0:HEADS, :], ACT.Exp).then_inc(s_dact, 1)
                act.wait_ge(s_dvec, 3)
                nc.scalar.activation(sp_e, sp_n, ACT.Exp).then_inc(s_dact, 1)
                act.wait_ge(s_dvec, 4)
                nc.scalar.activation(sp_n, sp_e, ACT.Ln).then_inc(s_dact, 1)
                act.wait_ge(s_k, 8 + 2 * LEVELS)
                act.sem_inc(s_silu, 2)

                def last_tap(q, s, j, by_tile):
                    tile = GT * (2 * q + s) + j
                    if by_tile:
                        act.wait_ge(s_tile, j + 1)
                    act.wait_ge(s_silu, tile + 1)
                    nc.scalar.activation(acc[:, j % 2, :], PS[:, GT * s + j, :], ACT.Copy,
                                         scale=tap_of(CONV - 1, tile)).then_inc(s_tap, 1)

                def silu(q, s, groups_before, by_tile=False):
                    if not by_tile:
                        act.wait_ge(s_grp, 2 * q + FLAT + s + 1)
                    last_tap(q, s, 0, by_tile)
                    for j in range(GT):
                        if j + 1 < GT:
                            last_tap(q, s, j + 1, by_tile)
                        act.wait_ge(s_bank[s], GT * (groups_before + q) + j + 1)
                        nc.scalar.activation(qkvT[:, bass.ds(GT * (2 * q + s) + j, 1), :].rearrange("p a t -> p (a t)"),
                                             acc[:, j % 2, :], ACT.Silu).then_inc(s_silu, 1)

                def pair(q, last):
                    split(2 * q + FLAT + 1)
                    silu(q, 0, FLAT // 2)
                    if not last:
                        split(2 * q + FLAT + 2)
                    silu(q, 1, FLAT // 2, last)

                with act.Fori(0, QKV_GROUPS // 2 - 1) as q:
                    pair(q, False)
                pair(QKV_GROUPS // 2 - 1, True)

            @block.vector
            def _(dve):
                steps = [0]

                def link(ins):
                    steps[0] = steps[0] + 1
                    ins.then_inc(s_v, 1)
                    dve.wait_ge(s_v, steps[0])

                def variance(t):
                    dve.wait_ge(s_sq, t + 1)
                    nc.vector.tensor_scalar(stat[:, 1, t:t + 1], stat[:, 0, t:t + 1], 1.0 / D, EPS, ALU.mult,
                                            ALU.add).then_inc(s_var, 1)

                dve.wait_ge(s_colT, 1)
                nc.vector.tensor_copy(cols[:, :], PS[:, 7, 0:P]).then_inc(s_col, 1)
                dve.wait_ge(s_col, 1)
                variance(0)
                for t in range(TT):
                    if t + 1 < TT:
                        variance(t + 1)
                    dve.wait_ge(s_std, t + 1)
                    link(nc.vector.reciprocal(stat[:, 0, t:t + 1], stat[:, 2, t:t + 1]))
                    nc.vector.tensor_scalar(x_rows[:, t, :], x_rows[:, t, :], stat[:, 0, t:t + 1], None,
                                            ALU.mult).then_inc(s_xs, 1)

                def turned(tiles):
                    for k in tiles:
                        dve.wait_ge(s_xh, k + 1)
                        nc.vector.scalar_tensor_tensor(out=xT_lo[:, k, :], in0=PS[:, k, :], scalar=mix_gain(k),
                                                       in1=xT_hi[:, k, :].bitcast(F32), op0=ALU.mult,
                                                       op1=ALU.subtract).then_inc(s_xl, 1)

                def split(g, parts=range(2)):
                    for kq in parts:
                        dve.wait_ge(s_h, 2 * g + kq + 1)
                        nc.vector.tensor_tensor(lo[:, kq, :, :], raw[:, kq, :, :], hi[:, kq, :, :].bitcast(F32),
                                                ALU.subtract).then_inc(s_l, 1)

                split(0, [0])
                turned(range(KD))
                split(0, [1])
                dve.wait_ge(s_abh, 1)
                nc.vector.tensor_tensor(wab_lo[:], wab_raw[:], wab_hi[:].bitcast(F32), ALU.subtract).then_inc(s_abl, 1)
                for g in range(FLAT):
                    split(g + 1)
                    if g in (2, 5):
                        dve.wait_ge(s_grp, g + 1)
                        dve.wait_ge(s_bank[0], GT * (1 if g == 2 else 3))
                        dve.wait_ge(s_bank[1], GT * (1 if g == 2 else 2))
                        for j in range(GT):
                            c = GT * (g // 3) + j
                            m, a = mprod[:, 0, :], acc[:, 0, :]
                            nc.vector.tensor_tensor(m, PS[:, GT * (g % 2) + j, :], ybT[:, c, :],
                                                    ALU.mult).then_inc(s_bank[g % 2], 1)
                            dve.wait_ge(s_bank[g % 2], GT * (g // 2) + j + 1)
                            link(nc.vector.tensor_scalar(a, m, sconv_tap(SCONV - 1, c), None, ALU.mult))
                            for s in range(1, SCONV):
                                link(nc.vector.scalar_tensor_tensor(
                                    out=a[:, s:], in0=m[:, :SEQ - s], scalar=sconv_tap(SCONV - 1 - s, c),
                                    in1=a[:, s:], op0=ALU.mult, op1=ALU.add))
                            nc.vector.tensor_tensor(ybT[:, c, :], a, gbT[:, j, :], ALU.mult).then_inc(s_yb, 1)
                            dve.wait_ge(s_yb, c + 1)
                    if g >= 6:
                        dve.wait_ge(s_const, 48)
                        for j in range(GT):
                            dve.wait_ge(s_bank[g % 2], GT * (g // 2) + j + 1)
                            c = GT * (g - 6) + j
                            nc.vector.tensor_scalar(zT[:, c, :], zT[:, c, :], gdn_gain[:, 0:1], None,
                                                    ALU.mult).then_inc(s_z, 1)

                a_rows = ab[0:HEADS, :]
                dve.wait_ge(s_ab, 1)
                nc.vector.tensor_scalar(sp_s, a_rows, dt_bias[0:HEADS, 0:1], None, ALU.add).then_inc(s_dvec, 1)
                dve.wait_ge(s_dvec, 1)
                nc.vector.tensor_scalar(sp_e, sp_s, -1.0, None, ALU.mult).then_inc(s_dvec, 1)
                dve.wait_ge(s_dvec, 2)
                nc.vector.tensor_tensor(sp_n, sp_s, sp_e, ALU.min).then_inc(s_dvec, 1)
                dve.wait_ge(s_dact, 2)
                nc.vector.tensor_scalar(sp_e, sp_e, 1.0, None, ALU.add).then_inc(s_dvec, 1)
                dve.wait_ge(s_dact, 3)
                nc.vector.scalar_tensor_tensor(out=sp_s, in0=sp_s, scalar=0.0, in1=sp_n, op0=ALU.max,
                                               op1=ALU.add).then_inc(s_dvec, 1)
                dve.wait_ge(s_dvec, 5)
                nc.vector.tensor_scalar(a_rows, sp_s, decay_rate[0:HEADS, 0:1], -1.0, ALU.mult,
                                        ALU.mult).then_inc(s_abr, 1)

                def conv(q, s, groups_before):
                    for j in range(GT):
                        tile = GT * (2 * q + s) + j
                        a, src = acc[:, j % 2, :], PS[:, GT * s + j, :]
                        dve.wait_ge(s_tap, tile + 1)
                        first = steps[0] + (CONV - 2) * tile
                        for d in range(1, CONV):
                            if d > 1:
                                dve.wait_ge(s_v, first + d - 1)
                            ins = nc.vector.scalar_tensor_tensor(
                                out=a[:, d:], in0=src[:, :SEQ - d], scalar=tap_of(CONV - 1 - d, tile),
                                in1=a[:, d:], op0=ALU.mult, op1=ALU.add)
                            ins.then_inc(s_v if d < CONV - 1 else s_bank[s], 1)

                def pair(q, last):
                    split(2 * q + FLAT + 1)
                    conv(q, 0, FLAT // 2)
                    if not last:
                        split(2 * q + FLAT + 2)
                    conv(q, 1, FLAT // 2)

                with dve.Fori(0, QKV_GROUPS // 2 - 1) as q:
                    pair(q, False)
                pair(QKV_GROUPS // 2 - 1, True)

            @block.tensor
            def _(pe):
                pe.wait_ge(s_k, 5)
                pe.wait_ge(s_rows, 48)
                pe.transpose(PS[:, 7, 0:P], small_rows[:, :], ident[:, :]).then_inc(s_colT, 1)
                pe.wait_ge(s_col, 1)
                for t in range(TT):
                    pe.wait_ge(s_xs, t + 1)
                    for k in range(KD):
                        mm = pe.transpose(PS[:, k, t * P:(t + 1) * P], x_rows[:, t, k * P:(k + 1) * P], ident[:, :])
                        if t == TT - 1:
                            mm.then_inc(s_xT, 1)

                def group(g, s):
                    for kq in range(2):
                        pe.wait_ge(s_l, 2 * g + kq + 1)
                        for kk in range(GT):
                            k = GT * kq + kk
                            if isinstance(g, int) and g == 0:
                                pe.wait_ge(s_xl, max(k + 1, GT))
                            for j in range(GT):
                                w_hi, w_lo = hi[:, kq, kk, j * P:(j + 1) * P], lo[:, kq, kk, j * P:(j + 1) * P]
                                dst = PS[:, GT * s + j, :]
                                pe.matmul(dst, w_hi, xT_hi[:, k, :], start=(k == 0), stop=False)
                                pe.matmul(dst, w_hi, xT_lo[:, k, :], start=False, stop=False)
                                mm = pe.matmul(dst, w_lo, xT_hi[:, k, :], start=False, stop=(k == KD - 1))
                                if k == KD - 1 and j == GT - 1:
                                    mm.then_inc(s_grp, 1)
                                elif kk == GT - 1 and j == GT - 1:
                                    mm.then_inc(s_used, 1)

                for g in range(FLAT):
                    wait(pe, s_bank[g % 2], GT * (g // 2))
                    group(g, g % 2)
                pe.wait_ge(s_bank[0], GT * (FLAT // 2))
                pe.wait_ge(s_abl, 1)
                for k in range(KD):
                    pe.matmul(PS[:, 0, :], wab_hi[:, k, :], xT_hi[:, k, :], start=(k == 0), stop=False)
                    pe.matmul(PS[:, 0, :], wab_hi[:, k, :], xT_lo[:, k, :], start=False, stop=False)
                    mm = pe.matmul(PS[:, 0, :], wab_lo[:, k, :], xT_hi[:, k, :], start=False, stop=(k == KD - 1))
                mm.then_inc(s_abp, 1)
                pe.wait_ge(s_ab, 1)
                with pe.Fori(0, QKV_GROUPS // 2 - 1) as q:
                    for s in range(2):
                        pe.wait_ge(s_bank[s], GT * (FLAT // 2) + GT * q)
                        group(2 * q + FLAT + s, s)
                q = QKV_GROUPS // 2 - 1
                pe.wait_ge(s_bank[0], GT * (FLAT // 2) + GT * q)
                group(2 * q + FLAT, 0)
                pe.wait_ge(s_bank[1], GT * (FLAT // 2) + GT * q)
                for kq, j in [(0, j) for j in range(GT)] + [(1, j) for j in range(GT)]:
                    pe.wait_ge(s_l, 2 * (2 * q + FLAT + 1) + kq + 1)
                    for k in range(GT * kq, GT * (kq + 1)):
                        w_hi, w_lo = (w[:, k // GT, k % GT, j * P:(j + 1) * P] for w in (hi, lo))
                        pe.matmul(PS[:, GT + j, :], w_hi, xT_hi[:, k, :], start=(k == 0), stop=False)
                        pe.matmul(PS[:, GT + j, :], w_hi, xT_lo[:, k, :], start=False, stop=False)
                        mm = pe.matmul(PS[:, GT + j, :], w_lo, xT_hi[:, k, :], start=False, stop=(k == KD - 1))
                    if kq == 1:
                        mm.then_inc(s_tile, 1)
        p1_psum.close()
        p1.close()
        HS = HEADS // 2
        BOTH = range(2)
        p2 = ExitStack()

        def p2_sb(name, shape, dt=F32):
            return p2.enter_context(nc.sbuf_tensor(name, shape, dt))

        stage = p2_sb("stage", [P, QKV, P])
        qn = p2_sb("qn", [P, HEADS, P])
        kn = p2_sb("kn", [P, HEADS, P])
        kb = p2_sb("kb", [P, HEADS, P])
        kd = p2_sb("kd", [P, HEADS, P])
        vb = p2_sb("vb", [P, HEADS, P])
        qT = p2_sb("qT", [P, HEADS, P])
        kT = p2_sb("kT", [P, HEADS, P])
        kbT = p2_sb("kbT", [P, HEADS, P])
        dec = p2_sb("dec", [P, HEADS, P])
        decs = p2_sb("decs", [P, HEADS, P])
        LT = p2_sb("LT", [P, HEADS, P])
        aqkT = p2_sb("aqkT", [P, HEADS, P])
        T = p2_sb("T", [P, HEADS, P])
        U = p2_sb("U", [P, HEADS, P])
        state = p2_sb("state", [P, HEADS, P])
        gtok = p2_sb("gtok", [P, TT, HEADS])
        btok = p2_sb("btok", [P, TT, HEADS])
        norms = p2_sb("norms", [P, 4, 2 * HEADS])
        gates = p2_sb("gates", [P, 8, HEADS])
        r = p2_sb("r", [P, HEADS, P])
        o = p2_sb("o", [P, HEADS, P])
        Y = kb
        MT = (qn, kn)
        vnew = T
        gbc = kbT
        sq_k, sq_q = LT, kbT
        gc, eg, egl, ekd, eb = (gates[:, n, :] for n in range(5))
        o_norm = gates[:, 5:8, :]

        def heads(tile, g):
            return tile[:, HS * g:HS * (g + 1), :]

        def wide(small):
            return small.unsqueeze(2).to_broadcast([P, small.shape[1], P])

        def of_chunk(by_token, c):
            if isinstance(c, int):
                return by_token[:, c, :]
            return by_token[:, bass.ds(c, 1), :].rearrange("p a h -> p (a h)")

        def each(mask):
            return mask.unsqueeze(1).to_broadcast([P, HS, P])

        s_tokT = mixer_sem("s_gates_turned")
        s_tok = mixer_sem("s_gates_by_token")
        s_stage = mixer_sem("s_stage_loaded")
        s_tq, s_tk, s_tv = mixer_sem("s_q_turned"), mixer_sem("s_k_turned"), mixer_sem("s_v_turned")
        s_sqr_k, s_sqr_q, s_red_k, s_red_q = (mixer_sem("s_k_squared"), mixer_sem("s_q_squared"),
                                              mixer_sem("s_k_summed"), mixer_sem("s_q_summed"))
        s_pow, s_powin = mixer_sem("s_qk_norms"), mixer_sem("s_qk_norms_asked")
        s_gbc, s_gcum, s_gcb = mixer_sem("s_g_spread"), mixer_sem("s_gcum"), mixer_sem("s_gcum_rows")
        s_gc, s_diff, s_exp = mixer_sem("s_gcum_copied"), mixer_sem("s_decay_diff"), mixer_sem("s_decay_exp")
        s_small, s_sexp, s_eb = mixer_sem("s_last_diff"), mixer_sem("s_small_exps"), mixer_sem("s_beta_decay")
        s_dect, s_decs = mixer_sem("s_decay_causal"), mixer_sem("s_decay_strict")
        s_vb, s_qn, s_kn, s_kb, s_kd = mixer_sem("s_vb"), mixer_sem("s_qn"), mixer_sem("s_kn"), mixer_sem("s_kb"), mixer_sem("s_kd")
        s_bq, s_bk, s_bkb = mixer_sem("s_q_back"), mixer_sem("s_k_back"), mixer_sem("s_kb_back")
        s_qT, s_kT, s_kbT = mixer_sem("s_qT"), mixer_sem("s_kT"), mixer_sem("s_kbT")
        s_G, s_A = mixer_sem("s_kk_products"), mixer_sem("s_qk_products")
        s_LT, s_AT = mixer_sem("s_LT"), mixer_sem("s_aqkT")
        s_MT = mixer_sem("s_level_mask")
        s_U, s_UT, s_T = mixer_sem("s_U"), mixer_sem("s_U_turned"), mixer_sem("s_T")
        s_Yp, s_Y, s_PT = mixer_sem("s_Y_product"), mixer_sem("s_Y"), mixer_sem("s_PT_product")
        s_kS, s_r1, s_r, s_qS, s_oS = mixer_sem("s_k_state"), mixer_sem("s_r_part"), mixer_sem("s_r"), mixer_sem("s_q_state"), mixer_sem("s_o_state")
        s_vn, s_vnew, s_oa, s_o = mixer_sem("s_v_new_product"), mixer_sem("s_v_new"), mixer_sem("s_o_product"), mixer_sem("s_o")
        s_Sd, s_Sp, s_S = mixer_sem("s_state_decayed"), mixer_sem("s_state_product"), mixer_sem("s_state")
        s_osq, s_ored, s_opin, s_opow, s_on = (mixer_sem("s_o_squared"), mixer_sem("s_o_summed"), mixer_sem("s_o_norm_asked"),
                                               mixer_sem("s_o_norm"), mixer_sem("s_o_scaled"))
        s_oT, s_chunk = mixer_sem("s_o_turned"), mixer_sem("s_chunk_done")
        s_half = mixer_sem("s_minus_half")
        s_v2, s_v3, s_v4 = mixer_sem("s_vector_decays"), mixer_sem("s_vector_norms"), mixer_sem("s_vector_gated")

        def column_source(weights, first):
            return weights.rearrange("(k p) c -> p k c", p=P)[:, :, first:first + GW]

        SOURCES = [column_source(w_in_d, GA0), column_source(w_in_d, GBB0),
                   column_source(w_in_d, GA0 + GW), column_source(w_in_d, GBB0 + GW)]
        for weights in (w_o_gdn[0], w_o_sconv[0], w_mix_out[0]):
            SOURCES += [column_source(weights, 0), column_source(weights, GW)]
        raw3 = qkvT[:, 0:2 * GT, :].rearrange("p (q k) c -> p q k c", q=2)
        t_raw = [sem(f"s_raw3_loaded{k}") for k in range(2)]

        p2_psum = ExitStack()
        PB = p2_psum.enter_context(nc.psum_tensor("PB", [P, 8, HS, P], F32))
        minus_half = p2_sb("minus_half", [P, 2 * HEADS])

        with nc.Block() as block:
            @block.sync
            def _(sp):
                sp.dma_start(stage[:], qkvT[:, :, P:2 * P]).then_inc(s_stage, 16)
                with sp.Fori(2, TT) as c:
                    sp.wait_ge(s_tv, 2 * c)
                    sp.dma_start(stage[:], qkvT[:, :, bass.ds(c * P, P)]).then_inc(s_stage, 16)
                sp.wait_ge(s_stage, 16 * (TT - 1))
                for kq in range(2):
                    sp.dma_start(raw3[:, kq, :, :], SOURCES[0][:, kq * GT:(kq + 1) * GT, :]).then_inc(t_raw[kq], 16)

            @block.gpsimd
            def _(pool):
                nc.gpsimd.memset(minus_half[:], -0.5).then_inc(s_half, 1)
                pool.wait_ge(s_half, 1)
                def decay_masks(c, g):
                    pool.wait_ge(s_exp, 2 * c + g + 1)
                    nc.gpsimd.tensor_tensor(heads(decs, g), heads(dec, g), each(strict[:]), ALU.mult).then_inc(s_decs, 1)
                    pool.wait_ge(s_decs, 2 * c + g + 1)
                    nc.gpsimd.tensor_tensor(heads(dec, g), heads(dec, g), each(tri[:]), ALU.mult).then_inc(s_dect, 1)

                def qk_norms(c):
                    pool.wait_ge(s_powin, c + 1)
                    nc.gpsimd.tensor_tensor(norms[:, 2, :], norms[:, 1, :], minus_half[:], ALU.pow).then_inc(s_pow, 1)

                def o_norms(c):
                    pool.wait_ge(s_opin, c + 1)
                    nc.gpsimd.tensor_tensor(o_norm[:, 2, :], o_norm[:, 1, :], minus_half[:, 0:HEADS],
                                            ALU.pow).then_inc(s_opow, 1)

                def middle(c):
                    for g in BOTH:
                        pool.wait_ge(s_kn, 2 * c + g + 1)
                        pool.wait_ge(s_sexp, 3 * c + 3)
                        nc.gpsimd.tensor_tensor(heads(kd, g), heads(kn, g), wide(ekd[:, HS * g:HS * (g + 1)]),
                                                ALU.mult).then_inc(s_kd, 1)
                    for lv in range(LEVELS):
                        for g in BOTH:
                            if lv == 0:
                                pool.wait_ge(s_LT, 2 * c + g + 1)
                                pool.wait_ge(s_qT, 2 * c + g + 1)
                            if lv == 1:
                                pool.wait_ge(s_kT, 2 * c + g + 1)
                                pool.wait_ge(s_kd, 2 * c + g + 1)
                            if lv == 2:
                                pool.wait_ge(s_U, 2 * LEVELS * c + g + 1)
                            if lv >= 3:
                                pool.wait_ge(s_Yp, 2 * (LEVELS - 1) * c + 2 * (lv - 3) + g + 1)
                            nc.gpsimd.tensor_tensor(heads(MT[lv % 2], g), heads(LT, g), each(pair_mask[:, lv, :]),
                                                    ALU.mult).then_inc(s_MT, 1)
                    for g in BOTH:
                        pool.wait_ge(s_r1, 2 * c + g + 1)
                        pool.wait_ge(s_oS, 2 * c + g + 1)
                        nc.gpsimd.tensor_tensor(heads(state, g), heads(state, g), wide(egl[:, HS * g:HS * (g + 1)]),
                                                ALU.mult).then_inc(s_Sd, 1)

                decay_masks(0, 0)
                qk_norms(0)
                decay_masks(0, 1)
                with pool.Fori(0, TT - 1) as c:
                    middle(c)
                    decay_masks(c + 1, 0)
                    qk_norms(c + 1)
                    decay_masks(c + 1, 1)
                    o_norms(c)
                middle(TT - 1)
                o_norms(TT - 1)

            @block.scalar
            def _(act):
                def exps(c):
                    for g in BOTH:
                        act.wait_ge(s_diff, 2 * c + g + 1)
                        nc.scalar.activation(heads(dec, g), heads(dec, g), ACT.Exp).then_inc(s_exp, 1)

                def small_exps(c):
                    act.wait_ge(s_gc, c + 1)
                    nc.scalar.activation(eg, gc, ACT.Exp).then_inc(s_sexp, 1)
                    act.wait_ge(s_small, 2 * c + 2)
                    nc.scalar.activation(egl, egl, ACT.Exp).then_inc(s_sexp, 1)
                    nc.scalar.activation(ekd, ekd, ACT.Exp).then_inc(s_sexp, 1)

                def squares(c, bank, dst, turned, done):
                    for g in BOTH:
                        act.wait_ge(turned, 2 * c + g + 1)
                        nc.scalar.activation(heads(dst, g), PB[:, bank + g], ACT.Square).then_inc(done, 1)

                def o_squares(c, k_summed):
                    for g in BOTH:
                        act.wait_ge(s_red_k, 2 * k_summed + g + 1)
                        act.wait_ge(s_o, 2 * c + g + 1)
                        nc.scalar.activation(heads(sq_k, g), heads(o, g), ACT.Square).then_inc(s_osq, 1)

                def values(c):
                    b_c = of_chunk(btok, c)
                    act.wait_ge(s_tok, 2)
                    for g in BOTH:
                        act.wait_ge(s_tv, 2 * c + g + 1)
                        for h in range(HS * g, HS * (g + 1)):
                            ins = nc.scalar.activation(vb[:, h, :], PB[:, 6 + g, h - HS * g, :], ACT.Copy,
                                                       scale=b_c[:, h:h + 1])
                        ins.then_inc(s_vb, 1)

                def new_values(c):
                    for g in BOTH:
                        act.wait_ge(s_vn, 2 * c + g + 1)
                        nc.scalar.activation(heads(vnew, g), PB[:, 2 + g], ACT.Copy).then_inc(s_vnew, 1)

                def middle(c):
                    for bank, src, dst, done in ((4, s_bk, kT, s_kT), (0, s_bq, qT, s_qT)):
                        for g in BOTH:
                            act.wait_ge(src, 2 * c + g + 1)
                            nc.scalar.activation(heads(dst, g), PB[:, bank + g], ACT.Copy).then_inc(done, 1)
                    for g in BOTH:
                        act.wait_ge(s_UT, 2 * (LEVELS - 1) * c + g + 1)
                        nc.scalar.activation(heads(T, g), PB[:, 4 + g], ACT.Copy).then_inc(s_T, 1)
                    for lv in range(1, LEVELS):
                        for g in BOTH:
                            act.wait_ge(s_Yp, 2 * (LEVELS - 1) * c + 2 * (lv - 1) + g + 1)
                            nc.scalar.activation(heads(Y, g), PB[:, g], ACT.Copy).then_inc(s_Y, 1)
                        if lv < LEVELS - 1:
                            for g in BOTH:
                                act.wait_ge(s_UT, 2 * (LEVELS - 1) * c + 2 * lv + g + 1)
                                nc.scalar.activation(heads(T, g), PB[:, 4 + g], ACT.Copy).then_inc(s_T, 1)

                squares(0, 4, sq_k, s_tk, s_sqr_k)
                squares(0, 0, aqkT, s_tq, s_sqr_q)
                exps(0)
                small_exps(0)
                values(0)

                def step(c):
                    middle(c)
                    squares(c + 1, 4, sq_k, s_tk, s_sqr_k)
                    exps(c + 1)
                    new_values(c)
                    squares(c + 1, 0, sq_q, s_tq, s_sqr_q)
                    small_exps(c + 1)
                    values(c + 1)
                    o_squares(c, c + 1)

                step(0)
                with act.Fori(1, TT - 1) as c:
                    step(c)
                middle(TT - 1)
                new_values(TT - 1)
                o_squares(TT - 1, TT - 1)

            @block.vector
            def _(dve):
                dve.wait_ge(s_tokT, 1)
                turned = PB[:, 6].rearrange("p (t h) c -> p t (h c)", t=TT)
                nc.vector.tensor_copy(gtok[:], turned[:, :, 0:HEADS]).then_inc(s_tok, 1)
                nc.vector.tensor_copy(btok[:], turned[:, :, 32:32 + HEADS]).then_inc(s_tok, 1)
                dve.wait_ge(s_tok, 2)

                def spread(c):
                    nc.vector.tensor_copy(gbc[:], wide(of_chunk(gtok, c))).then_inc(s_gbc, 1)

                def summed(c):
                    dve.wait_ge(s_gcum, c + 1)
                    nc.vector.tensor_copy(gc, PB[:, 7, 0, 0:HEADS]).then_inc(s_gc, 1)

                def decays(c):
                    dve.wait_ge(s_gc, c + 1)
                    for g in BOTH:
                        dve.wait_ge(s_gcb, 2 * c + g + 1)
                        if not (isinstance(c, int) and c == 0):
                            dve.wait_ge(s_kd, 2 * c + g - 1)
                            dve.wait_ge(s_Sd, 2 * c + g - 1)
                        hs = slice(HS * g, HS * (g + 1))
                        last = PB[:, 6 + g, :, P - 1]
                        nc.vector.tensor_copy(egl[:, hs], last).then_inc(s_v2, 1)
                        nc.vector.tensor_tensor(ekd[:, hs], last, gc[:, hs], ALU.subtract).then_inc(s_small, 1)
                        nc.vector.tensor_tensor(heads(dec, g), PB[:, 6 + g], wide(gc[:, hs]), ALU.subtract).then_inc(s_v2, 1)
                        dve.wait_ge(s_v2, 4 * c + 2 * g + 2)
                        nc.vector.tensor_scalar(heads(dec, g), heads(dec, g), 0.0, None, ALU.min).then_inc(s_diff, 1)

                def sums(c, squared, first, sq, done):
                    for g in BOTH:
                        dve.wait_ge(squared, 2 * c + g + 1)
                        nc.vector.tensor_reduce(norms[:, 0, first + HS * g:first + HS * (g + 1)], heads(sq, g), AX,
                                                ALU.add).then_inc(done, 1)

                def ask_norms(c):
                    dve.wait_ge(s_red_q, 2 * c + 2)
                    dve.wait_ge(s_red_k, 2 * c + 2)
                    nc.vector.tensor_scalar(norms[:, 1, 0:HEADS], norms[:, 0, 0:HEADS], EPS, float(P), ALU.add,
                                            ALU.mult).then_inc(s_v3, 1)
                    dve.wait_ge(s_v3, c + 1)
                    nc.vector.tensor_scalar(norms[:, 1, HEADS:], norms[:, 0, HEADS:], EPS, None,
                                            ALU.add).then_inc(s_powin, 1)

                def beta_decays(c):
                    b_c = of_chunk(btok, c)
                    dve.wait_ge(s_sexp, 3 * c + 3)
                    nc.vector.tensor_tensor(eb, eg, b_c, ALU.mult).then_inc(s_eb, 1)

                def normalised(c):
                    b_c = of_chunk(btok, c)
                    dve.wait_ge(s_pow, c + 1)
                    for g in BOTH:
                        hs = slice(HS * g, HS * (g + 1))
                        nc.vector.tensor_tensor(heads(kn, g), PB[:, 4 + g],
                                                wide(norms[:, 2, HEADS + HS * g:HEADS + HS * (g + 1)]),
                                                ALU.mult).then_inc(s_kn, 1)
                        nc.vector.tensor_tensor(heads(qn, g), PB[:, g], wide(norms[:, 2, hs]), ALU.mult).then_inc(s_qn, 1)
                        dve.wait_ge(s_kn, 2 * c + g + 1)
                        nc.vector.tensor_tensor(heads(kb, g), heads(kn, g), wide(b_c[:, hs]), ALU.mult).then_inc(s_kb, 1)

                def middle(c, before=True, more=True):
                    for g in BOTH:
                        dve.wait_ge(s_bkb, 2 * c + g + 1)
                        nc.vector.tensor_copy(heads(kbT, g), PB[:, 6 + g]).then_inc(s_kbT, 1)
                    for g in BOTH:
                        dve.wait_ge(s_G, 2 * c + g + 1)
                        dve.wait_ge(s_decs, 2 * c + g + 1)
                        nc.vector.tensor_tensor(heads(LT, g), PB[:, 4 + g], heads(decs, g), ALU.mult).then_inc(s_LT, 1)
                    for g in BOTH:
                        dve.wait_ge(s_A, 2 * c + g + 1)
                        dve.wait_ge(s_dect, 2 * c + g + 1)
                        nc.vector.tensor_tensor(heads(aqkT, g), PB[:, g], heads(dec, g), ALU.mult).then_inc(s_AT, 1)
                    for g in BOTH:
                        dve.wait_ge(s_MT, 2 * LEVELS * c + g + 1)
                        nc.vector.tensor_tensor(heads(U, g), each(ident[:]), heads(MT[0], g), ALU.subtract).then_inc(s_U, 1)
                    if before:
                        scale_o(c - 1)
                    for lv in range(1, LEVELS):
                        for g in BOTH:
                            hs = slice(HS * g, HS * (g + 1))
                            if lv == 1:
                                dve.wait_ge(s_kS, 2 * c + g + 1)
                                dve.wait_ge(s_eb, c + 1)
                                nc.vector.tensor_tensor(heads(r, g), PB[:, 6 + g], wide(eb[:, hs]), ALU.mult).then_inc(s_r1, 1)
                                dve.wait_ge(s_r1, 2 * c + g + 1)
                                dve.wait_ge(s_vb, 2 * c + g + 1)
                                nc.vector.tensor_tensor(heads(r, g), heads(vb, g), heads(r, g), ALU.subtract).then_inc(s_r, 1)
                            if lv == 2:
                                dve.wait_ge(s_qS, 2 * c + g + 1)
                                nc.vector.tensor_tensor(heads(o, g), PB[:, 6 + g], wide(eg[:, hs]),
                                                        ALU.mult).then_inc(s_oS, 1)
                        if before and lv == 1:
                            gate_o(c - 1)
                        if more and lv == 2:
                            spread(c + 1)
                        if more and lv == 3:
                            summed(c + 1)
                        if more and lv == LEVELS - 1:
                            decays(c + 1)
                        for g in BOTH:
                            dve.wait_ge(s_PT, 2 * (LEVELS - 1) * c + 2 * (lv - 1) + g + 1)
                            dve.wait_ge(s_U, 2 * LEVELS * c + 2 * (lv - 1) + g + 1)
                            nc.vector.tensor_tensor(heads(U, g), heads(U, g), PB[:, 2 + g], ALU.subtract).then_inc(s_U, 1)

                def outputs(c):
                    for g in BOTH:
                        dve.wait_ge(s_oa, 2 * c + g + 1)
                        dve.wait_ge(s_oS, 2 * c + g + 1)
                        nc.vector.tensor_tensor(heads(o, g), PB[:, 6 + g], heads(o, g), ALU.add).then_inc(s_o, 1)

                def new_state(c):
                    for g in BOTH:
                        dve.wait_ge(s_Sp, 2 * c + g + 1)
                        dve.wait_ge(s_Sd, 2 * c + g + 1)
                        nc.vector.tensor_tensor(heads(state, g), heads(state, g), PB[:, 2 + g], ALU.add).then_inc(s_S, 1)

                def ask_o_norms(c):
                    for g in BOTH:
                        dve.wait_ge(s_osq, 2 * c + g + 1)
                        nc.vector.tensor_reduce(o_norm[:, 0, HS * g:HS * (g + 1)], heads(sq_k, g), AX,
                                                ALU.add).then_inc(s_ored, 1)
                    dve.wait_ge(s_ored, 2 * c + 2)
                    nc.vector.tensor_scalar(o_norm[:, 1, :], o_norm[:, 0, :], 1.0 / P, EPS, ALU.mult,
                                            ALU.add).then_inc(s_opin, 1)

                def scale_o(c):
                    dve.wait_ge(s_opow, c + 1)
                    for g in BOTH:
                        nc.vector.tensor_tensor(heads(o, g), heads(o, g), wide(o_norm[:, 2, HS * g:HS * (g + 1)]),
                                                ALU.mult).then_inc(s_on, 1)

                def gate_o(c):
                    for g in BOTH:
                        dve.wait_ge(s_oT, 2 * c + g + 1)
                        gate = zT[:, HS * g:HS * (g + 1), bass.ds(c * P, P)]
                        ins = nc.vector.tensor_tensor(gate, PB[:, 2 + g], gate, ALU.mult)
                        ins.then_inc(s_chunk, 1) if g == 1 else ins.then_inc(s_v4, 1)

                spread(0)
                summed(0)
                nc.vector.memset(state[:], 0.0).then_inc(s_S, 2)
                nc.vector.memset(o_norm, 0.0).then_inc(s_chunk, 1)
                sums(0, s_sqr_k, HEADS, sq_k, s_red_k)
                sums(0, s_sqr_q, 0, aqkT, s_red_q)
                ask_norms(0)
                decays(0)
                normalised(0)
                beta_decays(0)

                def step(c, before=True):
                    middle(c, before)
                    sums(c + 1, s_sqr_k, HEADS, sq_k, s_red_k)
                    sums(c + 1, s_sqr_q, 0, sq_q, s_red_q)
                    ask_norms(c + 1)
                    outputs(c)
                    new_state(c)
                    normalised(c + 1)
                    ask_o_norms(c)
                    beta_decays(c + 1)

                step(0, before=False)
                with dve.Fori(1, TT - 1) as c:
                    step(c)
                middle(TT - 1, more=False)
                outputs(TT - 1)
                new_state(TT - 1)
                ask_o_norms(TT - 1)
                scale_o(TT - 1)
                gate_o(TT - 1)

            @block.tensor
            def _(pe):
                for t in range(TT):
                    mm = pe.transpose(PB[:, 6, t, :], ab[:, t * P:(t + 1) * P], ident[:, :])
                mm.then_inc(s_tokT, 1)

                def turn(bank, g, src, first):
                    for h in range(HS):
                        mm = pe.transpose(PB[:, bank + g, h, :], src[:, first + HS * g + h, :], ident[:, :])
                    return mm

                def product(bank, g, lhsT, rhs):
                    for h in range(HS):
                        mm = pe.matmul(PB[:, bank + g, h, :], lhsT[:, HS * g + h, :], rhs[:, HS * g + h, :],
                                       start=True, stop=True)
                    return mm

                def decays(c):
                    pe.wait_ge(s_gbc, c + 1)
                    g_c = gtok[:, c, :] if isinstance(c, int) else gtok[:, bass.ds(c, 1), :].rearrange("p a h -> p (a h)")
                    pe.matmul(PB[:, 7, 0, 0:HEADS], tri[:, :], g_c, start=True, stop=True).then_inc(s_gcum, 1)
                    decay_rows(c, 0)

                def decay_rows(c, g):
                    if g == 1:
                        pe.wait_ge(s_gc, c + 1)
                    for h in range(HS):
                        mm = pe.matmul(PB[:, 6 + g, h, :], gbc[:, HS * g + h, :], tri[:, :], start=True, stop=True)
                    mm.then_inc(s_gcb, 1)

                def turn_k(g, src):
                    turn(4, g, src, HEADS).then_inc(s_tk, 1)

                def turn_q(src):
                    for g in BOTH:
                        turn(0, g, src, 0).then_inc(s_tq, 1)

                def turn_v(src):
                    for g in BOTH:
                        turn(6, g, src, 2 * HEADS).then_inc(s_tv, 1)

                def turn_back(c):
                    for g in BOTH:
                        pe.wait_ge(s_kn, 2 * c + g + 1)
                        turn(4, g, kn, 0).then_inc(s_bk, 1)
                        pe.wait_ge(s_qn, 2 * c + g + 1)
                        turn(0, g, qn, 0).then_inc(s_bq, 1)
                        pe.wait_ge(s_kb, 2 * c + g + 1)
                        pe.wait_ge(s_vb, 2 * c + g + 1)
                        turn(6, g, kb, 0).then_inc(s_bkb, 1)

                def middle(c, before=True, more=True):
                    for g in BOTH:
                        pe.wait_ge(s_kT, 2 * c + g + 1)
                        pe.wait_ge(s_kbT, 2 * c + g + 1)
                        product(4, g, kT, kbT).then_inc(s_G, 1)
                        pe.wait_ge(s_qT, 2 * c + g + 1)
                        product(0, g, kT, qT).then_inc(s_A, 1)
                    for g in BOTH:
                        pe.wait_ge(s_S, 2 * c + g + 1)
                        product(6, g, kT, state).then_inc(s_kS, 1)
                    for g in BOTH:
                        pe.wait_ge(s_U, 2 * LEVELS * c + g + 1)
                        turn(4, g, U, 0).then_inc(s_UT, 1)
                    if before:
                        turn_o(c - 1)
                    for lv in range(1, LEVELS):
                        n = 2 * (LEVELS - 1) * c + 2 * (lv - 1)
                        for g in BOTH:
                            if lv == 1:
                                pe.wait_ge(s_AT, 2 * c + g + 1)
                            pe.wait_ge(s_T, n + g + 1)
                            pe.wait_ge(s_MT, 2 * LEVELS * c + 2 * lv + g + 1)
                            product(0, g, MT[lv % 2], T).then_inc(s_Yp, 1)
                        if lv == 1:
                            for g in BOTH:
                                pe.wait_ge(s_r1, 2 * c + g + 1)
                                product(6, g, qT, state).then_inc(s_qS, 1)
                            pe.wait_ge(s_chunk, c + 1)
                        if more and lv == 3:
                            pe.wait_ge(s_oS, 2 * c + 2)
                            decays(c + 1)
                        if more and lv == 4:
                            decay_rows(c + 1, 1)
                        if more and lv == LEVELS - 1:
                            pe.wait_ge(s_stage, 16 * (c + 1))
                            turn_k(0, stage)
                        for g in BOTH:
                            pe.wait_ge(s_Y, n + g + 1)
                            product(2, g, Y, U).then_inc(s_PT, 1)
                        if more and lv == LEVELS - 1:
                            turn_k(1, stage)
                        if lv < LEVELS - 1:
                            for g in BOTH:
                                pe.wait_ge(s_U, 2 * LEVELS * c + 2 * lv + g + 1)
                                turn(4, g, U, 0).then_inc(s_UT, 1)

                def new_values(c):
                    for g in BOTH:
                        pe.wait_ge(s_U, 2 * LEVELS * c + 2 * (LEVELS - 1) + g + 1)
                        pe.wait_ge(s_r, 2 * c + g + 1)
                        product(2, g, U, r).then_inc(s_vn, 1)

                def outputs(c, free, value):
                    for g in BOTH:
                        pe.wait_ge(free, value + g)
                        pe.wait_ge(s_vnew, 2 * c + g + 1)
                        product(6, g, aqkT, vnew).then_inc(s_oa, 1)

                def new_state(c):
                    for g in BOTH:
                        pe.wait_ge(s_kd, 2 * c + g + 1)
                        product(2, g, kd, vnew).then_inc(s_Sp, 1)

                def turn_o(c):
                    for g in BOTH:
                        pe.wait_ge(s_S, 2 * c + g + 3)
                        pe.wait_ge(s_on, 2 * c + g + 1)
                        turn(2, g, o, 0).then_inc(s_oT, 1)

                first = qkvT[:, :, 0:P]
                turn_k(0, first)
                turn_k(1, first)
                turn_q(first)
                pe.wait_ge(s_tok, 2)
                decays(0)
                decay_rows(0, 1)
                pe.wait_ge(s_diff, 2)
                turn_v(first)
                turn_back(0)

                def step(c, before=True):
                    middle(c, before)
                    turn_q(stage)
                    new_values(c)
                    outputs(c, s_diff, 2 * c + 3)
                    new_state(c)
                    pe.wait_ge(s_o, 2 * c + 2)
                    turn_v(stage)
                    turn_back(c + 1)

                step(0, before=False)
                with pe.Fori(1, TT - 1) as c:
                    step(c)
                middle(TT - 1, more=False)
                new_values(TT - 1)
                outputs(TT - 1, s_oS, 2 * TT - 1)
                new_state(TT - 1)
                turn_o(TT - 1)
        p2_psum.close()
        p2.close()
        p3 = ExitStack()

        def p3_sb(name, shape, dt=F32):
            return p3.enter_context(nc.sbuf_tensor(name, shape, dt))

        out_hi = p3_sb("out_hi", [P, KD, SEQ], F32R)
        out_lo = p3_sb("out_lo", [P, KD, SEQ], F32R)
        gateA = qkvT[:, 2 * GT:2 * GT + KD, :]
        gateB = qkvT[:, 2 * GT + KD:2 * GT + 2 * KD, :]
        hi3 = p3_sb("hi3", [P, 2, GT, GW], F32R)
        lo3 = p3_sb("lo3", [P, 2, GT, GW], F32R)
        part = p3_sb("part", [P, 2, SEQ])
        h_rows = zT[:].rearrange("p a b -> p (a b)").rearrange("p (t d) -> p t d", t=TT)
        xn2 = gateB.rearrange("p a b -> p (a b)").rearrange("p (t d) -> p t d", t=TT)
        xn2T = gateA
        ffn_gain = raw3[:, 0, 0:2, :].rearrange("p a c -> p (a c)")
        router_w = raw3[:, 1, 0, 0:KD * E].rearrange("p (k e) -> p k e", k=KD)
        router_b = raw3[:, 1, 1, 0:E]
        sq3 = ybT[:, 0:2, :].rearrange("p a b -> p (a b)")
        stat3 = ybT[:, 2, 0:16].rearrange("p (n t) -> p n t", n=4)

        N3 = len(SOURCES)
        GATES, YA, YB, MIX = 0, 4, 6, 8

        t_h, t_l, t_used, t_grp = sem("s_hi3_ready"), sem("s_lo3_ready"), sem("s_chunk3_used"), sem("s_group3_done")
        t_bank = [sem(f"s_banks3_read{k}") for k in range(2)]
        s_oh, s_ol = sem("s_o_hi"), sem("s_o_lo")
        s_yh, s_yl = sem("s_yb_hi"), sem("s_yb_lo")
        s_merge, s_mh, s_ml = sem("s_merged"), sem("s_merged_hi"), sem("s_merged_lo")
        s_xr = sem("s_x_reloaded")
        s_hrow = sem("s_h_rows")
        s_small3 = sem("s_router_loaded")
        s_sq3, s_var3, s_std3, s_xn2 = sem("s_h_squared"), sem("s_h_variance"), sem("s_h_std"), sem("s_xn2_ready")
        s_xn2T, s_xn2c = sem("s_xn2_turned"), sem("s_xn2T_ready")
        s_logit, s_v5, s_store = sem("s_logits"), sem("s_vector_highest"), sem("s_xn2_stored")
        s_tile3, s_rstd3 = sem("s_mix_tile_done"), sem("s_h_rstd")

        p3_psum = ExitStack()
        PS3 = p3_psum.enter_context(nc.psum_tensor("PS3", [P, 2 * GT, GW], F32))
        nc.clear_and_free_semaphores(mixer_sems)

        with nc.Block() as block:
            @block.sync
            def _(sp):
                for g in range(1, N3):
                    for kq in range(2):
                        sp.wait_ge(t_l, 2 * g + kq - 1)
                        sp.dma_start(raw3[:, kq, :, :], SOURCES[g][:, kq * GT:(kq + 1) * GT, :]).then_inc(t_raw[kq], 16)
                    if g == YA:
                        sp.wait_ge(s_ol, KD)
                        sp.dma_start(h_rows[:], x_d).then_inc(s_xr, 16)
                sp.wait_ge(t_l, 2 * N3)
                sp.dma_start(ffn_gain, norm_ffn_g[0].partition_broadcast(P)).then_inc(s_small3, 16)
                sp.dma_start(router_w, w_router[0].rearrange("(k p) e -> p k e", p=P)).then_inc(s_small3, 16)
                sp.dma_start(router_b, b_router[0].partition_broadcast(P)).then_inc(s_small3, 16)
                for t in range(TT):
                    sp.wait_ge(s_xn2, t + 1)
                    sp.dma_start(xn2_d.rearrange("(t p) d -> p t d", p=P)[:, t, :], xn2[:, t, :]).then_inc(s_store, 16)
                sp.wait_ge(s_store, 16 * TT)
            @block.scalar
            def _(act):
                def split(g):
                    for kq in range(2):
                        act.wait_ge(t_raw[kq], 16 * (g + 1))
                        wait(act, t_grp if kq else t_used, g)
                        nc.scalar.activation(hi3[:, kq, :, :], raw3[:, kq, :, :], ACT.Copy).then_inc(t_h, 1)

                split(0)
                for g in range(N3):
                    if g + 1 < N3:
                        split(g + 1)
                    if g == GATES + 1:
                        for k in range(KD):
                            nc.scalar.activation(out_hi[:, k, :], zT[:, k, :], ACT.Copy).then_inc(s_oh, 1)
                    if g < YA:
                        act.wait_ge(t_grp, g + 1)
                        gate = (gateA, gateB)[g % 2]
                        for j in range(GT):
                            nc.scalar.activation(gate[:, GT * (g // 2) + j, :], PS3[:, GT * (g % 2) + j, :],
                                                 ACT.Sigmoid).then_inc(t_bank[g % 2], 1)
                    if g == YA - 1:
                        for k in range(KD):
                            nc.scalar.activation(xT_hi[:, k, :], ybT[:, k, :], ACT.Copy).then_inc(s_yh, 1)
                    if YB <= g < MIX:
                        for j in range(GT):
                            k = GT * (g - YB) + j
                            act.wait_ge(s_merge, k + 1)
                            nc.scalar.activation(out_hi[:, k, :], gateA[:, k, :], ACT.Copy).then_inc(s_mh, 1)

                def turned(t):
                    act.wait_ge(s_xn2T, t + 1)
                    for q in range(2):
                        nc.scalar.activation(xn2T[:, GT * q:GT * (q + 1), t * P:(t + 1) * P],
                                             PS3[:, 2 * (t % 2) + q, :].rearrange("p (k s) -> p k s", s=P),
                                             ACT.Copy).then_inc(s_xn2c, 1)

                for t in range(TT):
                    act.wait_ge(s_hrow, TT + t + 1)
                    wait(act, s_sq3, t)
                    nc.scalar.activation(sq3, h_rows[:, t, :], ACT.Square, accum_out=stat3[:, 0, t:t + 1]).then_inc(s_sq3, 1)
                    act.wait_ge(s_var3, t + 1)
                    nc.scalar.activation(stat3[:, 2, t:t + 1], stat3[:, 1, t:t + 1], ACT.Sqrt).then_inc(s_std3, 1)
                    if t >= 1:
                        turned(t - 1)
                turned(TT - 1)

            @block.vector
            def _(dve):
                def second_norm(t):
                    column = [stat3[:, n, t:t + 1] for n in range(4)]
                    dve.wait_ge(s_sq3, t + 1)
                    nc.vector.tensor_scalar(column[1], column[0], 1.0 / D, EPS, ALU.mult, ALU.add).then_inc(s_var3, 1)
                    dve.wait_ge(s_std3, t + 1)
                    nc.vector.reciprocal(column[3], column[2]).then_inc(s_rstd3, 1)
                    dve.wait_ge(s_rstd3, t + 1)
                    dve.wait_ge(s_small3, 48)
                    nc.vector.scalar_tensor_tensor(out=xn2[:, t, :], in0=h_rows[:, t, :], scalar=column[3],
                                                   in1=ffn_gain, op0=ALU.mult, op1=ALU.mult).then_inc(s_xn2, 1)

                def highest(t):
                    dve.wait_ge(s_logit, t + 1)
                    nc.vector.tensor_tensor(logits[:, t, :], PS3[:, GT + t, 0:E], router_b, ALU.add).then_inc(s_v5, 1)
                    dve.wait_ge(s_v5, 3 * t + 1)
                    nc.vector.max(top[:, t, :], logits[:, t, :]).then_inc(s_v5, 1)
                    dve.wait_ge(s_v5, 3 * t + 2)
                    nc.vector.max_index(top_i[:, t, :], top[:, t, :], logits[:, t, :]).then_inc(s_v5, 1)

                def split(g):
                    for kq in range(2):
                        dve.wait_ge(t_h, 2 * g + kq + 1)
                        nc.vector.tensor_tensor(lo3[:, kq, :, :], raw3[:, kq, :, :], hi3[:, kq, :, :].bitcast(F32),
                                                ALU.subtract).then_inc(t_l, 1)

                split(0)
                for g in range(N3):
                    if g + 1 < N3:
                        split(g + 1)
                    if g == GATES + 1:
                        for k in range(KD):
                            dve.wait_ge(s_oh, k + 1)
                            nc.vector.tensor_tensor(out_lo[:, k, :], zT[:, k, :], out_hi[:, k, :].bitcast(F32),
                                                    ALU.subtract).then_inc(s_ol, 1)
                    if g == YA - 1:
                        for k in range(KD):
                            dve.wait_ge(s_yh, k + 1)
                            nc.vector.tensor_tensor(xT_lo[:, k, :], ybT[:, k, :], xT_hi[:, k, :].bitcast(F32),
                                                    ALU.subtract).then_inc(s_yl, 1)
                    if YA <= g <= MIX:
                        dve.wait_ge(t_grp, g + 1)
                    for j in range(GT):
                        k = GT * (g % 2) + j
                        bank = PS3[:, GT * (g % 2) + j, :]
                        if YA <= g < YB:
                            dve.wait_ge(t_bank[0], 2 * GT)
                            dve.wait_ge(t_bank[1], 2 * GT)
                            nc.vector.tensor_tensor(gateA[:, k, :], bank, gateA[:, k, :], ALU.mult).then_inc(t_bank[g % 2], 1)
                        elif YB <= g < MIX:
                            if k >= 2:
                                dve.wait_ge(s_merge, k - 1)
                            nc.vector.tensor_tensor(part[:, j % 2, :], bank, gateB[:, k, :], ALU.mult).then_inc(t_bank[g % 2], 1)
                            dve.wait_ge(t_bank[g % 2], GT * (g // 2) + j + 1)
                            nc.vector.tensor_tensor(gateA[:, k, :], gateA[:, k, :], part[:, j % 2, :],
                                                    ALU.add).then_inc(s_merge, 1)
                            dve.wait_ge(s_mh, k + 1)
                            nc.vector.tensor_tensor(out_lo[:, k, :], gateA[:, k, :], out_hi[:, k, :].bitcast(F32),
                                                    ALU.subtract).then_inc(s_ml, 1)
                        elif g >= MIX:
                            dve.wait_ge(s_xr, 16)
                            if g == MIX + 1:
                                dve.wait_ge(s_tile3, j + 1)
                            rows = h_rows[:, j, GW * (g - MIX):GW * (g - MIX + 1)]
                            nc.vector.tensor_tensor(rows, rows, bank, ALU.add).then_inc(s_hrow, 1)
                            if g == MIX + 1:
                                second_norm(j)
                                if j >= 2:
                                    highest(j - 2)
                for t in range(TT - 2, TT):
                    highest(t)

            @block.tensor
            def _(pe):
                def turn_row_tile(t):
                    pe.wait_ge(s_xn2, t + 1)
                    pe.wait_ge(s_hrow, TT)
                    wait(pe, s_xn2c, 2 * (t - 1))
                    for k in range(KD):
                        mm = pe.transpose(PS3[:, 2 * (t % 2) + k // GT, (k % GT) * P:(k % GT + 1) * P],
                                          xn2[:, t, k * P:(k + 1) * P], ident[:, :])
                    mm.then_inc(s_xn2T, 1)

                def router(t):
                    pe.wait_ge(s_xn2c, 2 * (t + 1))
                    for k in range(KD):
                        mm = pe.matmul(PS3[:, GT + t, 0:E], xn2T[:, k, t * P:(t + 1) * P], router_w[:, k, :],
                                       start=(k == 0), stop=(k == KD - 1))
                    mm.then_inc(s_logit, 1)

                for g in range(N3 - 1):
                    if g < MIX:
                        wait(pe, t_bank[g % 2], GT * (g // 2))
                    else:
                        pe.wait_ge(t_bank[g % 2], GT * (MIX // 2))
                    if g == YA:
                        pe.wait_ge(s_ol, KD)
                    if g == YB:
                        pe.wait_ge(s_yl, KD)
                    r_hi, r_lo = (out_hi, out_lo) if YA <= g < YB else (xT_hi, xT_lo)
                    for kq in range(2):
                        pe.wait_ge(t_l, 2 * g + kq + 1)
                        for kk in range(GT):
                            k = GT * kq + kk
                            if g == MIX:
                                pe.wait_ge(s_ml, k + 1)
                            for j in range(GT):
                                dst = PS3[:, GT * (g % 2) + j, :]
                                if g < MIX:
                                    w_hi, w_lo = (w[:, kq, kk, j * P:(j + 1) * P] for w in (hi3, lo3))
                                    terms = ((w_hi, r_hi[:, k, :]), (w_hi, r_lo[:, k, :]), (w_lo, r_hi[:, k, :]))
                                else:
                                    m_hi, m_lo = (m[:, k, j * P:(j + 1) * P] for m in (out_hi, out_lo))
                                    terms = ((m_hi, hi3[:, kq, kk, :]), (m_hi, lo3[:, kq, kk, :]), (m_lo, hi3[:, kq, kk, :]))
                                for n, (lhsT, rhs) in enumerate(terms):
                                    mm = pe.matmul(dst, lhsT, rhs, start=(k == 0 and n == 0), stop=(k == KD - 1 and n == 2))
                                if k == KD - 1 and j == GT - 1:
                                    mm.then_inc(t_grp, 1)
                                elif kk == GT - 1 and j == GT - 1:
                                    mm.then_inc(t_used, 1)
                pe.wait_ge(t_bank[1], GT * (MIX // 2))
                for kq, t in [(0, t) for t in range(TT)] + [(1, t) for t in range(TT)]:
                    pe.wait_ge(t_l, 2 * (N3 - 1) + kq + 1)
                    for k in range(GT * kq, GT * (kq + 1)):
                        m_hi, m_lo = (m[:, k, t * P:(t + 1) * P] for m in (out_hi, out_lo))
                        w_hi, w_lo = (w[:, k // GT, k % GT, :] for w in (hi3, lo3))
                        for n, (lhsT, rhs) in enumerate(((m_hi, w_hi), (m_hi, w_lo), (m_lo, w_hi))):
                            mm = pe.matmul(PS3[:, GT + t, :], lhsT, rhs, start=(k == 0 and n == 0),
                                           stop=(k == KD - 1 and n == 2))
                    if kq == 0:
                        continue
                    mm.then_inc(s_tile3, 1)
                    if t >= 1:
                        turn_row_tile(t - 1)
                    if t >= 2:
                        router(t - 2)
                router(TT - 2)
                turn_row_tile(TT - 1)
                router(TT - 1)
        p3_psum.close()
        p3.close()
        front.close()
        mixer.close()

        ITEMS = E * TT
        CH = 12
        RAW = 6
        SPL = 4
        EARLY = 1
        K4 = TT * TOPK

        y_d = nc.dram_tensor("expert_rows_scratch", (SEQ * TOPK + P, D), F32, kind="Internal").ap()

        mraw = keep("mraw", [P, RAW, 2, 2, GW])
        mhi = keep("mhi", [P, SPL, 2, 2, GW], F32R)
        mlo = keep("mlo", [P, SPL, 2, 2, GW], F32R)
        bias = keep("bias", [2 * E, 3 * D], F32R)
        pick = keep("pick", [2 * E, E + 1])
        ones_row = keep("ones_row", [2 * E, P])
        index = keep("index", [P, ITEMS + 1], U32)
        target = keep("target", [P, ITEMS], U32)
        weight = keep("weight", [P, K4])
        more_items = keep("more_items", [P, 1], I32)

        route = ExitStack()

        def r_sb(name, shape, dt=F32):
            return route.enter_context(nc.sbuf_tensor(name, shape, dt))

        bias_raw = r_sb("bias_raw", [2 * E, 3 * D])
        iota_i = r_sb("iota_i", [P, P + TT + K4], I32)
        iota = r_sb("iota", [P, P + TT + K4])
        target_f = r_sb("target_f", [P, 2, ITEMS])
        ones = r_sb("ones", [P, P])
        chosen = r_sb("chosen", [P, K4, E])
        taken = r_sb("taken", [P, TT, E])
        place = r_sb("place", [P, TT, E])
        at_place = r_sb("at_place", [P, K4, E])
        small = r_sb("small", [P, 12, K4])
        slot_is = r_sb("slot_is", [P, K4, P])
        item_is = r_sb("item_is", [P, K4, P])
        e_f, pos, blk, blk2, blk3, item, within, row, d4, ex4, tok4, sums = (small[:, n, :] for n in range(12))

        s_br, s_bh, s_bl = sem("s_bias_loaded"), sem("s_bias_hi"), sem("s_bias_lo")
        s_io, s_pk, s_on1 = sem("s_iotas"), sem("s_pick_ready"), sem("s_ones_ready")
        s_vr = sem("s_routing_step")
        s_taken, s_place, s_hot, s_idx = sem("s_taken_ready"), sem("s_places"), sem("s_one_hots"), sem("s_index_product")
        s_d4, s_ex4 = sem("s_top_diff"), sem("s_top_exp")
        e_h, e_l, e_used = sem("s_weights_hi"), sem("s_weights_lo"), sem("s_weights_used")
        s_mraw = [sem(f"s_weights_loaded{k}") for k in range(RAW)]

        PM = ctx.enter_context(nc.psum_tensor("PM", [P, 8, GW], F32))

        gu = w_gate_up[0].rearrange("e (q kk p) (two c) -> e q p kk two c", p=P, kk=2, two=2)
        dn = w_down[0].rearrange("e (q kk p) (two c) -> e q p kk two c", p=P, kk=2, two=2)

        def load_weights(sp, e, m):
            src, half = (gu, m // 4) if m < 8 else (dn, 0)
            for kk in range(2):
                one = src[bass.ds(e, 1), m % 4, :, kk].rearrange("a p two c -> (a p) two c")
                sp.dma_start(mraw[:, m % RAW, kk], one[:, :, half * GW:(half + 1) * GW]).then_inc(s_mraw[m % RAW], 16)

        with nc.Block() as block:
            @block.sync
            def _(sp):
                for half in range(2):
                    rows = slice(E * half, E * half + E)
                    sp.dma_start(bias_raw[rows, 0:2 * D], b_gate_up[0]).then_inc(s_br, 16)
                    sp.dma_start(bias_raw[rows, 2 * D:3 * D], b_down[0]).then_inc(s_br, 16)
                for m in range(RAW + EARLY):
                    wait(sp, e_l, m - RAW + 1)
                    load_weights(sp, 0, m)
            @block.gpsimd
            def _(pool):
                nc.gpsimd.iota(iota_i[:, 0:P], [[1, P]], base=0, channel_multiplier=0).then_inc(s_io, 1)
                nc.gpsimd.iota(iota_i[:, P:P + TT], [[0, TT]], base=SEQ * TOPK, channel_multiplier=1).then_inc(s_io, 1)
                nc.gpsimd.iota(iota_i[:, P + TT:], [[TOPK * P, TT], [1, TOPK]], base=0, channel_multiplier=TOPK).then_inc(s_io, 1)
                nc.gpsimd.memset(ones[:], 1.0).then_inc(s_on1, 1)
                nc.gpsimd.memset(index[:], 0).then_inc(s_on1, 1)
                nc.gpsimd.memset(ones_row[:], 1.0).then_inc(s_on1, 1)
                pool.wait_ge(s_on1, 3)
                for n, (rows, first, dst) in enumerate(((slice(0, E), 0, 0), (slice(E, 2 * E), E, 0))):
                    nc.gpsimd.tensor_copy(pick[rows, 0:E], ident[rows, first:first + E]).then_inc(s_pk, 1)
                    pool.wait_ge(s_pk, 2 * n + 1)
                    nc.gpsimd.tensor_copy(pick[rows, E:E + 1], ident[rows, first:first + 1]).then_inc(s_pk, 1)
                    pool.wait_ge(s_pk, 2 * n + 2)
                pool.wait_ge(s_bh, 1)
                nc.gpsimd.tensor_tensor(bias[E:2 * E, :], bias_raw[E:2 * E, :], bias[E:2 * E, :].bitcast(F32),
                                        ALU.subtract).then_inc(s_bl, 1)
                pool.wait_ge(s_bl, 1)
                for m in range(EARLY):
                    pool.wait_ge(e_h, m + 1)
                    nc.gpsimd.tensor_tensor(mlo[:, m], mraw[:, m], mhi[:, m].bitcast(F32), ALU.subtract).then_inc(e_l, 1)

            @block.scalar
            def _(act):
                act.wait_ge(s_br, 64)
                nc.scalar.activation(bias[:], bias_raw[:], ACT.Copy).then_inc(s_bh, 1)
                for m in range(EARLY):
                    act.wait_ge(s_mraw[m], 32)
                    nc.scalar.activation(mhi[:, m], mraw[:, m], ACT.Copy).then_inc(e_h, 1)
                act.wait_ge(s_d4, 1)
                nc.scalar.activation(ex4, d4, ACT.Exp).then_inc(s_ex4, 1)

            @block.vector
            def _(dve):
                steps = [0]

                def link(ins):
                    steps[0] += 1
                    ins.then_inc(s_vr, 1)
                    dve.wait_ge(s_vr, steps[0])

                def by_tile(tile):
                    return tile.rearrange("p (t k) -> p t k", t=TT)

                link(nc.vector.tensor_copy(by_tile(e_f), top_i[:, :, 0:TOPK]))
                dve.wait_ge(s_io, 3)
                link(nc.vector.tensor_copy(iota[:], iota_i[:]))
                link(nc.vector.tensor_tensor(chosen[:], iota[:, 0:E].unsqueeze(1).to_broadcast([P, K4, E]),
                                             e_f.unsqueeze(2).to_broadcast([P, K4, E]), ALU.is_equal))
                nc.vector.tensor_reduce(taken[:], chosen[:].rearrange("p (t k) e -> p t e k", t=TT), AX,
                                        ALU.add).then_inc(s_taken, 1)
                nc.vector.tensor_tensor(by_tile(d4), top[:, :, 0:TOPK], top[:, :, 0:1].to_broadcast([P, TT, TOPK]),
                                        ALU.subtract).then_inc(s_d4, 1)
                dve.wait_ge(s_place, 1)
                link(nc.vector.tensor_copy(place[:], PM[:, 0, 0:TT * E].rearrange("p (t e) -> p t e", t=TT)))
                link(nc.vector.tensor_reduce(sums[:, 8:9], PM[:, 1, 0:E], AX, ALU.max))
                link(nc.vector.tensor_scalar(sums[:, 9:10], sums[:, 8:9], float(P), None, ALU.is_gt))
                for n in range(2, TT):
                    link(nc.vector.scalar_tensor_tensor(out=sums[:, 9:10], in0=sums[:, 8:9], scalar=float(n * P),
                                                        in1=sums[:, 9:10], op0=ALU.is_gt, op1=ALU.add))
                link(nc.vector.tensor_copy(more_items[:], sums[:, 9:10]))
                link(nc.vector.tensor_tensor(at_place[:].rearrange("p (t k) e -> p t k e", t=TT),
                                             chosen[:].rearrange("p (t k) e -> p t k e", t=TT),
                                             place[:].unsqueeze(2).to_broadcast([P, TT, TOPK, E]), ALU.mult))
                link(nc.vector.tensor_reduce(pos, at_place[:], AX, ALU.add))
                link(nc.vector.tensor_scalar(blk, pos, float(P), None, ALU.is_ge))
                link(nc.vector.scalar_tensor_tensor(out=blk2, in0=pos, scalar=2.0 * P, in1=blk, op0=ALU.is_ge, op1=ALU.add))
                link(nc.vector.scalar_tensor_tensor(out=blk3, in0=pos, scalar=3.0 * P, in1=blk2, op0=ALU.is_ge, op1=ALU.add))
                link(nc.vector.scalar_tensor_tensor(out=item, in0=blk3, scalar=float(E), in1=e_f, op0=ALU.mult, op1=ALU.add))
                link(nc.vector.scalar_tensor_tensor(out=within, in0=blk3, scalar=-float(P), in1=pos, op0=ALU.mult, op1=ALU.add))
                link(nc.vector.scalar_tensor_tensor(out=row, in0=within, scalar=-1.0, in1=iota[:, P + TT:P + TT + K4],
                                                    op0=ALU.mult, op1=ALU.add))
                link(nc.vector.tensor_scalar(tok4, row, -float(SEQ * TOPK), None, ALU.add))
                for n in range(K4):
                    nc.vector.tensor_scalar(slot_is[:, n, :], iota[:, 0:P], within[:, n:n + 1], None,
                                            ALU.is_equal).then_inc(s_hot, 1)
                    nc.vector.tensor_scalar(item_is[:, n, :], iota[:, 0:P], item[:, n:n + 1], tok4[:, n:n + 1],
                                            ALU.is_equal, ALU.mult).then_inc(s_hot, 1)
                dve.wait_ge(s_ex4, 1)
                link(nc.vector.tensor_reduce(sums[:, 0:TT], by_tile(ex4), AX, ALU.add))
                link(nc.vector.reciprocal(sums[:, TT:2 * TT], sums[:, 0:TT]))
                link(nc.vector.tensor_tensor(by_tile(weight[:]), by_tile(ex4),
                                             sums[:, TT:2 * TT].unsqueeze(2).to_broadcast([P, TT, TOPK]), ALU.mult))
                dve.wait_ge(s_idx, 1)
                dve.wait_ge(s_on1, 3)
                link(nc.vector.tensor_scalar(target_f[:, 0, :], PM[:, 2, 0:ITEMS], iota[:, P:P + 1], None, ALU.add))
                link(nc.vector.tensor_copy(target[:], target_f[:, 0, :]))
                link(nc.vector.tensor_scalar(target_f[:, 1, :], target_f[:, 0, :], float(SEQ * TOPK - 1), None, ALU.min))
                link(nc.vector.tensor_copy(index[:, 0:ITEMS], target_f[:, 1, :]))
                link(nc.vector.tensor_scalar(index[:, 0:ITEMS], index[:, 0:ITEMS], 2, None, ALU.logical_shift_right))

            @block.tensor
            def _(pe):
                pe.wait_ge(s_taken, 1)
                pe.wait_ge(s_on1, 3)
                for t in range(TT):
                    for before in range(t + 1):
                        pe.matmul(PM[:, 0, t * E:(t + 1) * E], strict[:, :] if before == t else ones[:, :],
                                  taken[:, before, :], start=(before == 0), stop=(before == t))
                for t in range(TT):
                    mm = pe.matmul(PM[:, 1, 0:E], ones[:, :], taken[:, t, :], start=(t == 0), stop=(t == TT - 1))
                mm.then_inc(s_place, 1)
                for n in range(K4):
                    pe.wait_ge(s_hot, 2 * n + 2)
                    mm = pe.matmul(PM[:, 2, 0:ITEMS], slot_is[:, n, :], item_is[:, n, :], start=(n == 0), stop=(n == K4 - 1))
                mm.then_inc(s_idx, 1)
        route.close()

        expert = keep("expert", [2 * E, P], F32R)
        now = keep("now", [P, 2], U32)
        xg = keep("xg", [P, D])
        xgT_hi = keep("xgT_hi", [P, KD, P], F32R)
        xgT_lo = keep("xgT_lo", [P, KD, P], F32R)
        glu = keep("glu", [P, 2, 4, GW])
        hT_hi = keep("hT_hi", [P, KD, P], F32R)
        hT_lo = keep("hT_lo", [P, KD, P], F32R)
        y_rows = keep("y_rows", [P, D])
        idle = keep("idle", [P, 2])
        LIMIT, ALPHA = 7.0, 1.702
        HALF = KD // 2

        s_now, s_xg, s_tx = sem("s_index_copied"), sem("s_tokens_gathered"), sem("s_tokens_turned")
        s_gh, s_gl = sem("s_tokens_hi"), sem("s_tokens_lo")
        s_exp2 = sem("s_expert_picked")
        s_gate, s_up, s_sig, s_prod, s_hid = (sem("s_gate_clamped"), sem("s_up_clamped"), sem("s_gate_sigmoid"),
                                              sem("s_gate_times_up"), sem("s_hidden"))
        s_th, s_hh, s_hl = sem("s_hidden_turned"), sem("s_hidden_hi"), sem("s_hidden_lo")
        s_y, s_yst, s_goal = sem("s_y_rows"), sem("s_y_stored"), sem("s_target_copied")
        s_yfree, s_idle = sem("s_y_rows_free"), sem("s_idle_step")

        def last_item(eng):
            return eng.value_load(more_items[0:1, 0:1], min_val=0, max_val=TT - 1) * E + (E - 1)

        def all_items(eng, body):
            more = eng.value_load(more_items[0:1, 0:1], min_val=0, max_val=TT - 1)
            with eng.Fori(0, more + 1) as b:
                with eng.Fori(0, E) as e:
                    body(b * E + e, e)

        with nc.Block() as block:
            @block.sync
            def _(sp):
                last = last_item(sp)

                def load(i, m):
                    sp.wait_ge(e_l, CH * i + m - RAW + 1)
                    load_weights(sp, i % E, m)

                with sp.Fori(0, last) as i:
                    for m in range(RAW + EARLY, CH):
                        load(i, m)
                    for m in range(RAW + EARLY):
                        load(i + 1, m)
                for m in range(RAW + EARLY, CH):
                    sp.wait_ge(e_l, CH * last + m - RAW + 1)
                    load_weights(sp, E - 1, m)
                for m in range(3):
                    sp.wait_ge(e_l, CH * last + CH - RAW + m + 1)
                    sp.sem_inc(s_mraw[m], 32)

            @block.gpsimd
            def _(pool):
                def step():
                    nc.gpsimd.tensor_tensor(idle[:, 0:1], idle[:, 1:2], idle[:, 1:2], ALU.add).then_inc(s_idle, 1)

                nc.gpsimd.memset(idle[:], 0.0).then_inc(s_idle, 1)
                pool.wait_ge(s_idle, 1)
                pool.sem_inc(s_yfree, 1)

                def gather(i):
                    nc.gpsimd.tensor_copy(now[:, 0:1], index[:, bass.ds(i, 1)]).then_inc(s_now, 1)
                    pool.wait_ge(s_now, i + 1)
                    step()
                    nc.gpsimd.indirect_dma_start(xg[:], None, xn2_d, bass.IndirectOffsetOnAxis(ap=now[:, 0:1], axis=0)
                                                 ).then_inc(s_xg, 16)

                gather(0)

                def body(i, e):
                    pool.wait_ge(s_tx, i + 1)
                    gather(i + 1)
                    for half in range(2):
                        pool.wait_ge(s_prod, 2 * i + half + 1)
                        pool.wait_ge(s_sig, 2 * i + half + 1)
                        nc.gpsimd.tensor_tensor(glu[:, half, 3, :], glu[:, half, 1, :], glu[:, half, 2, :],
                                                ALU.mult).then_inc(s_hid, 1)
                    nc.gpsimd.tensor_copy(now[:, 1:2], target[:, bass.ds(i, 1)]).then_inc(s_goal, 1)
                    pool.wait_ge(s_goal, i + 1)
                    pool.wait_ge(s_y, 2 * i + 3)
                    step()
                    nc.gpsimd.indirect_dma_start(y_d, bass.IndirectOffsetOnAxis(ap=now[:, 1:2], axis=0), y_rows[:], None
                                                 ).then_inc(s_yst, 16)
                    pool.wait_ge(s_yst, 16 * i + 16)
                    pool.sem_inc(s_yfree, 1)

                all_items(pool, body)

            @block.scalar
            def _(act):
                act.sem_inc(e_used, SPL)
                act.sem_inc(s_y, 1)

                def split(i, m):
                    act.wait_ge(s_mraw[m % RAW], 64 * i + 32 * (m // RAW) + 32)
                    act.wait_ge(e_used, CH * i + m + 1)
                    nc.scalar.activation(mhi[:, m % SPL], mraw[:, m % RAW], ACT.Copy).then_inc(e_h, 1)

                def tokens_hi(i):
                    for q in range(2):
                        act.wait_ge(s_tx, i + 1)
                        nc.scalar.activation(xgT_hi[:, HALF * q:HALF * (q + 1), :], PM[:, q, :].rearrange("p (k s) -> p k s", s=P),
                                             ACT.Copy).then_inc(s_gh, 1)

                def sigmoid(i, half):
                    act.wait_ge(s_gate, 2 * i + half + 1)
                    nc.scalar.activation(glu[:, half, 2, :], glu[:, half, 0, :], ACT.Sigmoid, scale=ALPHA).then_inc(s_sig, 1)

                def hidden_hi(i, half):
                    act.wait_ge(s_th, 2 * i + half + 1)
                    nc.scalar.activation(hT_hi[:, HALF * half:HALF * (half + 1), :],
                                         PM[:, 6 + half, :].rearrange("p (k s) -> p k s", s=P), ACT.Copy).then_inc(s_hh, 1)

                nc.scalar.activation(expert[:], ones_row[:], ACT.Copy, scale=pick[:, 0:1]).then_inc(s_exp2, 1)
                for m in range(EARLY, 3):
                    split(0, m)
                tokens_hi(0)

                def body(i, e):
                    for m in range(3, 8):
                        split(i, m)
                    sigmoid(i, 0)
                    split(i, 8)
                    split(i, 9)
                    hidden_hi(i, 0)
                    split(i, 10)
                    split(i, 11)
                    sigmoid(i, 1)
                    split(i + 1, 0)
                    hidden_hi(i, 1)
                    tokens_hi(i + 1)
                    split(i + 1, 1)
                    split(i + 1, 2)
                    act.wait_ge(e_used, CH * (i + 1) + SPL)
                    nc.scalar.activation(expert[:], ones_row[:], ACT.Copy, scale=pick[:, bass.ds(e + 1, 1)]).then_inc(s_exp2, 1)
                    act.wait_ge(s_yfree, i + 1)
                    for half in range(2):
                        nc.scalar.activation(y_rows[:, GW * half:GW * (half + 1)], PM[:, 4 + half, :], ACT.Copy).then_inc(s_y, 1)

                all_items(act, body)

            @block.vector
            def _(dve):
                def split(i, m):
                    dve.wait_ge(e_h, CH * i + m + 1)
                    nc.vector.tensor_tensor(mlo[:, m % SPL], mraw[:, m % RAW], mhi[:, m % SPL].bitcast(F32),
                                            ALU.subtract).then_inc(e_l, 1)

                def tokens_lo(i):
                    for q in range(2):
                        dve.wait_ge(s_gh, 2 * i + q + 1)
                        part_of = slice(HALF * q, HALF * (q + 1))
                        nc.vector.tensor_tensor(xgT_lo[:, part_of, :], PM[:, q, :].rearrange("p (k s) -> p k s", s=P),
                                                xgT_hi[:, part_of, :].bitcast(F32), ALU.subtract).then_inc(s_gl, 1)

                def clamp(i, half):
                    dve.wait_ge(e_used, CH * i + 4 * (half + 1) + SPL)
                    nc.vector.tensor_scalar(glu[:, half, 0, :], PM[:, 2 * half, :], LIMIT, None, ALU.min).then_inc(s_gate, 1)
                    nc.vector.tensor_scalar(glu[:, half, 1, :], PM[:, 2 * half + 1, :], LIMIT, -LIMIT, ALU.min,
                                            ALU.max).then_inc(s_up, 1)

                def gated(i, half):
                    dve.wait_ge(s_up, 2 * i + half + 1)
                    nc.vector.scalar_tensor_tensor(out=glu[:, half, 1, :], in0=glu[:, half, 1, :], scalar=1.0,
                                                   in1=glu[:, half, 0, :], op0=ALU.add, op1=ALU.mult).then_inc(s_prod, 1)

                def hidden_lo(i, half):
                    dve.wait_ge(s_hh, 2 * i + half + 1)
                    part_of = slice(HALF * half, HALF * (half + 1))
                    nc.vector.tensor_tensor(hT_lo[:, part_of, :], PM[:, 6 + half, :].rearrange("p (k s) -> p k s", s=P),
                                            hT_hi[:, part_of, :].bitcast(F32), ALU.subtract).then_inc(s_hl, 1)

                for m in range(EARLY, 3):
                    split(0, m)
                tokens_lo(0)

                def body(i, e):
                    for m in range(3, 8):
                        split(i, m)
                    clamp(i, 0)
                    gated(i, 0)
                    split(i, 8)
                    hidden_lo(i, 0)
                    split(i, 9)
                    clamp(i, 1)
                    gated(i, 1)
                    split(i, 10)
                    split(i, 11)
                    hidden_lo(i, 1)
                    split(i + 1, 0)
                    tokens_lo(i + 1)
                    split(i + 1, 1)
                    split(i + 1, 2)

                all_items(dve, body)

            @block.tensor
            def _(pe):
                def turn_tokens(i):
                    pe.wait_ge(s_xg, 16 * i + 16)
                    for k in range(KD):
                        mm = pe.transpose(PM[:, k // HALF, (k % HALF) * P:(k % HALF + 1) * P], xg[:, k * P:(k + 1) * P], ident[:, :])
                    mm.then_inc(s_tx, 1)

                def turn_hidden(i, half):
                    pe.wait_ge(s_hid, 2 * i + half + 1)
                    for k in range(HALF):
                        mm = pe.transpose(PM[:, 6 + half, k * P:(k + 1) * P], glu[:, half, 3, k * P:(k + 1) * P], ident[:, :])
                    mm.then_inc(s_th, 1)

                def start_with_bias(bank, first):
                    for n in range(2):
                        pe.matmul(PM[:, bank + n, :], expert[:, :], bias[:, first[n]:first[n] + GW], start=True, stop=False)

                def chunk(i, m, bank, t_hi, t_lo):
                    pe.wait_ge(e_l, CH * i + m + 1)
                    w_hi, w_lo = mhi[:, m % SPL], mlo[:, m % SPL]
                    for kk in range(2):
                        k = 2 * (m % 4) + kk
                        for n in range(2):
                            pe.matmul(PM[:, bank + n, :], t_hi[:, k, :], w_hi[:, kk, n, :], start=False, stop=False)
                            pe.matmul(PM[:, bank + n, :], t_hi[:, k, :], w_lo[:, kk, n, :], start=False, stop=False)
                        for n in range(2):
                            mm = pe.matmul(PM[:, bank + n, :], t_lo[:, k, :], w_hi[:, kk, n, :], start=False, stop=(k == KD - 1))
                    mm.then_inc(e_used, 1)

                turn_tokens(0)

                def body(i, e):
                    pe.wait_ge(s_gl, 2 * i + 2)
                    pe.wait_ge(s_exp2, i + 1)
                    start_with_bias(0, (0, D))
                    for m in range(4):
                        chunk(i, m, 0, xgT_hi, xgT_lo)
                    start_with_bias(2, (GW, D + GW))
                    for m in range(4, 7):
                        chunk(i, m, 2, xgT_hi, xgT_lo)
                    turn_hidden(i, 0)
                    chunk(i, 7, 2, xgT_hi, xgT_lo)
                    pe.wait_ge(s_y, 2 * i + 1)
                    start_with_bias(4, (2 * D, 2 * D + GW))
                    pe.wait_ge(s_hl, 2 * i + 1)
                    chunk(i, 8, 4, hT_hi, hT_lo)
                    chunk(i, 9, 4, hT_hi, hT_lo)
                    turn_hidden(i, 1)
                    turn_tokens(i + 1)
                    pe.wait_ge(s_hl, 2 * i + 2)
                    chunk(i, 10, 4, hT_hi, hT_lo)
                    chunk(i, 11, 4, hT_hi, hT_lo)

                all_items(pe, body)

        rows_t = [mraw[:, 2 * n:2 * n + 2].rearrange("p s a b c -> p (s a b c)").rearrange("p (k d) -> p k d", k=TOPK)
                  for n in range(RAW // 2)]
        AHEAD = len(rows_t)
        final_gain = glu[:, 0, 2:4, :].rearrange("p b c -> p (b c)")
        y_by_token = y_d[0:SEQ * TOPK, :].rearrange("(t p k) d -> t p (k d)", p=P, k=TOPK)
        s_fg, s_pick = sem("s_final_gain"), [[sem(f"s_rows_back{t}{half}") for half in range(2)] for t in range(TT)]
        s_added, s_fsq, s_fvar, s_fstd, s_frec, s_out, s_st = (
            sem("s_row_added"), sem("s_final_squares"), sem("s_final_variance"), sem("s_final_std"),
            sem("s_final_rstd"), sem("s_out_ready"), sem("s_out_stored"))
        fstat = glu[:, 0, 0, 0:16].rearrange("p (n t) -> p n t", n=4)
        fsq = glu[:, 1, 0:2, :].rearrange("p a c -> p (a c)")

        with nc.Block() as block:
            @block.sync
            def _(sp):
                sp.dma_start(final_gain, norm_final_g.partition_broadcast(P)).then_inc(s_fg, 16)
                sp.wait_ge(s_yst, last_item(sp) * 16 + 16)
                for t in range(TT):
                    wait(sp, s_added, TOPK * (t - AHEAD + 1))
                    for half in range(2):
                        w = slice(half * 2 * D, (half + 1) * 2 * D)
                        sp.dma_start(rows_t[t % AHEAD].rearrange("p k d -> p (k d)")[:, w], y_by_token[t][:, w]
                                     ).then_inc(s_pick[t][half], 16)
                for t in range(TT):
                    sp.wait_ge(s_out, t + 1)
                    sp.dma_start(out_d[:, t, :], h_rows[:, t, :]).then_inc(s_st, 16)
                sp.wait_ge(s_st, 16 * TT)

            @block.scalar
            def _(act):
                for t in range(TT):
                    act.wait_ge(s_added, TOPK * (t + 1))
                    wait(act, s_fsq, t)
                    nc.scalar.activation(fsq, h_rows[:, t, :], ACT.Square, accum_out=fstat[:, 0, t:t + 1]).then_inc(s_fsq, 1)
                    act.wait_ge(s_fvar, t + 1)
                    nc.scalar.activation(fstat[:, 2, t:t + 1], fstat[:, 1, t:t + 1], ACT.Sqrt).then_inc(s_fstd, 1)

            @block.vector
            def _(dve):
                def finish(t):
                    dve.wait_ge(s_fsq, t + 1)
                    nc.vector.tensor_scalar(fstat[:, 1, t:t + 1], fstat[:, 0, t:t + 1], 1.0 / D, EPS, ALU.mult,
                                            ALU.add).then_inc(s_fvar, 1)
                    dve.wait_ge(s_fstd, t + 1)
                    nc.vector.reciprocal(fstat[:, 3, t:t + 1], fstat[:, 2, t:t + 1]).then_inc(s_frec, 1)
                    dve.wait_ge(s_frec, t + 1)
                    dve.wait_ge(s_fg, 16)
                    nc.vector.scalar_tensor_tensor(out=h_rows[:, t, :], in0=h_rows[:, t, :], scalar=fstat[:, 3, t:t + 1],
                                                   in1=final_gain, op0=ALU.mult, op1=ALU.mult).then_inc(s_out, 1)

                for t in range(TT):
                    for k in range(TOPK):
                        n = t * TOPK + k
                        dve.wait_ge(s_pick[t][k * 2 // TOPK], 16)
                        wait(dve, s_added, n)
                        nc.vector.scalar_tensor_tensor(out=h_rows[:, t, :], in0=rows_t[t % AHEAD][:, k, :],
                                                       scalar=weight[:, n:n + 1], in1=h_rows[:, t, :], op0=ALU.mult,
                                                       op1=ALU.add).then_inc(s_added, 1)
                    if t >= 1:
                        finish(t - 1)
                finish(TT - 1)


_INS = ["x", "norm_mix_g", "w_in", "gdn_conv_w", "gdn_A_log", "gdn_dt_bias", "gdn_norm_g", "w_o_gdn", "sconv_w",
        "w_o_sconv", "w_mix_out", "norm_ffn_g", "w_router", "b_router", "w_gate_up", "b_gate_up", "w_down",
        "b_down", "norm_final_g"]


def kernel(**inputs):
    import numpy as _np
    import concourse.bacc as _bacc
    from concourse.bass_utils import run_bass_kernel_spmd as _run

    nc = _bacc.Bacc("TRN2", target_bir_lowering=False, num_devices=1)
    arrays, args = {}, []
    for name in _INS:
        a = _np.ascontiguousarray(inputs[name])
        arrays[f"in_{name}_dram"] = a
        args.append(nc.dram_tensor(f"in_{name}_dram", a.shape, mybir.dt.from_np(a.dtype), kind="ExternalInput").ap())
    out = nc.dram_tensor("out_0_dram", inputs["x"].shape, F32, kind="ExternalOutput").ap()
    hybrid_block(nc, *args, out)
    r = _run(nc, [arrays], core_ids=[0])
    return r.results[0]["out_0_dram"]
```
